# Optimizing a Trainium2 kernel written in Bass

```python
import jax, jax.numpy as jnp
from jax import lax
import numpy as np

D_MODEL = 1024
BATCH = 1
SEQ = 512
DEPTH = 1
DEC_BATCH = 8
DEC_SEQ = 4
PAST_LEN = 4096
PAGE_SIZE = 128

MIX_WIDTH = 2 * D_MODEL
SSD_WIDTH = MIX_WIDTH // 2
SSD_HEAD_DIM = 64
SSD_HEADS = SSD_WIDTH // SSD_HEAD_DIM
SSD_GROUPS = 2
SSD_STATE = 64
SSD_CHUNK = 128
SSD_CONV_DIM = SSD_WIDTH + 2 * SSD_GROUPS * SSD_STATE
LRU_WIDTH = MIX_WIDTH - SSD_WIDTH
LRU_BLOCKS = 16
LRU_BLOCK_DIM = LRU_WIDTH // LRU_BLOCKS
LRU_C = 8.0
CONV_W = 4
IN_PROJ_DIM = SSD_WIDTH + SSD_CONV_DIM + SSD_HEADS + 2 * LRU_WIDTH
PEER_HEADS = 8
PEER_KEYS = 128
PEER_EXPERTS = PEER_KEYS * PEER_KEYS
PEER_TOPK = 16
PEER_QDIM = 256
PEER_HALF = PEER_QDIM // 2
PEER_BLOCK = 256
PLE_DIM = 256
EPS = 1e-6

kernel_name = 'hymba_ssd_rglru_peer_step'

def rmsnorm(x, g):
    xf = x.astype(jnp.float32)
    out = xf * lax.rsqrt(jnp.mean(xf * xf, axis=-1, keepdims=True) + EPS)
    return (out * g.astype(jnp.float32)).astype(x.dtype)

def causal_conv(x, buf, w, b):
    L = x.shape[1]
    xp = jnp.concatenate([buf.astype(x.dtype), x], axis=1)
    y = b + xp[:, 0:L] * w[0]
    for k in range(1, CONV_W):
        y = y + xp[:, k:k + L] * w[k]
    return y, xp[:, -(CONV_W - 1):]

def segsum(x):
    T = x.shape[-1]
    cs = jnp.cumsum(x, axis=-1)
    diff = cs[..., :, None] - cs[..., None, :]
    mask = jnp.tril(jnp.ones((T, T), dtype=bool))
    return jnp.where(mask, diff, -jnp.inf)

def ssd_chunked(xs, dt, a, bm, cm, h0):
    b, l, H, P = xs.shape
    q = min(SSD_CHUNK, l)
    c = l // q
    rep = H // SSD_GROUPS
    bh = jnp.repeat(bm, rep, axis=2).reshape(b, c, q, H, SSD_STATE)
    ch = jnp.repeat(cm, rep, axis=2).reshape(b, c, q, H, SSD_STATE)
    xdt = (xs * dt[..., None]).reshape(b, c, q, H, P)
    da = (dt * a).reshape(b, c, q, H).transpose(0, 3, 1, 2)
    a_cs = jnp.cumsum(da, axis=-1)
    scores = jnp.einsum('bclhn,bcshn->bhcls', ch, bh) * jnp.exp(segsum(da))
    y_diag = jnp.einsum('bhcls,bcshp->bclhp', scores, xdt)
    decay_states = jnp.exp(a_cs[..., -1:] - a_cs)
    states = jnp.einsum('bclhn,bhcl,bclhp->bchpn', bh, decay_states, xdt)
    states = jnp.concatenate([h0.astype(states.dtype)[:, None], states], axis=1)
    chunk_decay = jnp.exp(segsum(jnp.pad(a_cs[..., -1], ((0, 0), (0, 0), (1, 0)))))
    new_states = jnp.einsum('bhzc,bchpn->bzhpn', chunk_decay, states)
    prev_states, final = new_states[:, :-1], new_states[:, -1]
    y_off = jnp.einsum('bclhn,bchpn,bhcl->bclhp', ch, prev_states, jnp.exp(a_cs))
    return (y_diag + y_off).reshape(b, l, H, P), final

def lru_scan(a_t, bx, h0):
    bx = bx.at[:, 0].add(a_t[:, 0] * h0.astype(bx.dtype))

    def comb(c1, c2):
        a1, b1 = c1
        a2, b2 = c2
        return a1 * a2, a2 * b1 + b2

    _, hs = lax.associative_scan(comb, (a_t, bx), axis=1)
    return hs, hs[:, -1]

def peer(xn, wq, sub_keys, expert_u, expert_v):
    B_, L_, D = xn.shape
    t = xn.reshape(-1, D)
    T = t.shape[0]
    nb = -(-T // PEER_BLOCK)
    t = jnp.pad(t, ((0, nb * PEER_BLOCK - T), (0, 0))).reshape(nb, PEER_BLOCK, D)

    def block(tb):
        n = tb.shape[0]
        qv = (tb @ wq).reshape(n, PEER_HEADS, 2, PEER_HALF)
        s = jnp.einsum('thcd,hckd->thck', qv, sub_keys).astype(jnp.float32)
        s_top, i_top = lax.top_k(s, PEER_TOPK)
        cand = (s_top[:, :, 0, :, None] + s_top[:, :, 1, None, :]).reshape(n, PEER_HEADS, -1)
        cand_idx = (i_top[:, :, 0, :, None] * PEER_KEYS + i_top[:, :, 1, None, :]).reshape(n, PEER_HEADS, -1)
        best, pos = lax.top_k(cand, PEER_TOPK)
        idx = jnp.take_along_axis(cand_idx, pos, axis=-1)
        g = jax.nn.softmax(best, axis=-1).astype(tb.dtype)
        u = expert_u[idx]
        act = jax.nn.gelu(jnp.einsum('td,thkd->thk', tb, u))
        v = expert_v[idx]
        return jnp.einsum('thk,thkd->td', g * act, v)

    out = lax.map(block, t).reshape(-1, D)[:T]
    return out.reshape(B_, L_, D)

def layer(h, p, ssd_h0, ssd_buf, lru_h0, lru_buf, lw):
    b, l, _ = h.shape
    xn = rmsnorm(h, lw['norm_mix'])
    proj = xn @ lw['w_in']
    s1 = SSD_WIDTH
    s2 = s1 + SSD_CONV_DIM
    s3 = s2 + SSD_HEADS
    s4 = s3 + LRU_WIDTH
    z, xbc, dt, gate, xl = jnp.split(proj, [s1, s2, s3, s4], axis=-1)
    xbc, ssd_buf_new = causal_conv(xbc, ssd_buf, lw['conv_ssd_w'], lw['conv_ssd_b'])
    xbc = jax.nn.silu(xbc)
    xs, bm, cm = jnp.split(xbc, [SSD_WIDTH, SSD_WIDTH + SSD_GROUPS * SSD_STATE], axis=-1)
    xs = xs.reshape(b, l, SSD_HEADS, SSD_HEAD_DIM)
    bm = bm.reshape(b, l, SSD_GROUPS, SSD_STATE)
    cm = cm.reshape(b, l, SSD_GROUPS, SSD_STATE)
    dt = jax.nn.softplus(dt + lw['dt_bias'])
    a = -jnp.exp(lw['a_log'])
    y, ssd_h = ssd_chunked(xs, dt, a, bm, cm, ssd_h0)
    y = y + lw['d_skip'][:, None] * xs
    y_ssd = rmsnorm(y.reshape(b, l, SSD_WIDTH) * jax.nn.silu(z), lw['norm_ssd'])
    xl, lru_buf_new = causal_conv(xl, lru_buf, lw['conv_lru_w'], lw['conv_lru_b'])
    xb = xl.reshape(b, l, LRU_BLOCKS, LRU_BLOCK_DIM)
    r_gate = jax.nn.sigmoid(jnp.einsum('blki,kij->blkj', xb, lw['w_rgate']).reshape(b, l, LRU_WIDTH) + lw['b_rgate'])
    i_gate = jax.nn.sigmoid(jnp.einsum('blki,kij->blkj', xb, lw['w_igate']).reshape(b, l, LRU_WIDTH) + lw['b_igate'])
    log_a = -LRU_C * r_gate * jax.nn.softplus(-lw['lru_lambda'])
    a_t = jnp.exp(log_a)
    mult = jnp.sqrt(-jnp.expm1(2.0 * log_a))
    hs, lru_h = lru_scan(a_t, mult * (i_gate * xl), lru_h0)
    y_lru = rmsnorm(hs * jax.nn.gelu(gate), lw['norm_lru'])
    h = h + jnp.concatenate([y_ssd, y_lru], axis=-1) @ lw['w_out']
    h = h + peer(rmsnorm(h, lw['norm_ffn']), lw['peer_wq'], lw['peer_keys'], lw['peer_u'], lw['peer_v'])
    g = jax.nn.sigmoid(rmsnorm(h, lw['norm_ple_gate']) @ lw['w_ple_gate'])
    h = h + rmsnorm((p @ lw['w_ple_proj']) * g, lw['norm_ple_out'])
    return h, ssd_h, ssd_buf_new, lru_h, lru_buf_new

def setup_inputs(seed: int = 0) -> dict:
    key = jax.random.key(seed)
    ks = jax.random.split(key, 40)
    f32 = jnp.float32

    def nrm(k, shape, scale):
        return jax.random.normal(k, shape, f32) * scale

    def gain(k, shape):
        return 1.0 + 0.02 * jax.random.normal(k, shape, f32)

    u_dt = jax.random.uniform(ks[0], (DEPTH, SSD_HEADS), f32)
    dt0 = jnp.exp(u_dt * (np.log(0.1) - np.log(0.001)) + np.log(0.001))
    dt_bias = dt0 + jnp.log(-jnp.expm1(-dt0))
    a_log = jnp.log(jax.random.uniform(ks[1], (DEPTH, SSD_HEADS), f32, minval=1.0, maxval=16.0))
    u_lam = jax.random.uniform(ks[2], (DEPTH, LRU_WIDTH), f32, minval=0.9, maxval=0.999)
    a_base = u_lam ** (1.0 / LRU_C)
    lru_lambda = jnp.log(a_base) - jnp.log1p(-a_base)

    return {
        'x_prompt': nrm(ks[3], (BATCH, SEQ, D_MODEL), 1.0),
        'x_sample': nrm(ks[4], (DEC_BATCH, DEC_SEQ, D_MODEL), 1.0),
        'state_ssd': nrm(ks[5], (DEPTH, DEC_BATCH, SSD_HEADS, SSD_HEAD_DIM, SSD_STATE), 0.5),
        'state_ssd_conv': nrm(ks[6], (DEPTH, DEC_BATCH, CONV_W - 1, SSD_CONV_DIM), 1.0),
        'state_lru': nrm(ks[7], (DEPTH, DEC_BATCH, LRU_WIDTH), 0.5),
        'state_lru_conv': nrm(ks[8], (DEPTH, DEC_BATCH, CONV_W - 1, LRU_WIDTH), 1.0),
        'p_prompt': nrm(ks[9], (DEPTH, BATCH, SEQ, PLE_DIM), 1.0),
        'p_sample': nrm(ks[10], (DEPTH, DEC_BATCH, DEC_SEQ, PLE_DIM), 1.0),
        'norm_mix': gain(ks[11], (DEPTH, D_MODEL)),
        'w_in': nrm(ks[12], (DEPTH, D_MODEL, IN_PROJ_DIM), D_MODEL ** -0.5),
        'conv_ssd_w': nrm(ks[13], (DEPTH, CONV_W, SSD_CONV_DIM), CONV_W ** -0.5),
        'conv_ssd_b': nrm(ks[14], (DEPTH, SSD_CONV_DIM), 0.02),
        'dt_bias': dt_bias,
        'a_log': a_log,
        'd_skip': gain(ks[15], (DEPTH, SSD_HEADS)),
        'norm_ssd': gain(ks[16], (DEPTH, SSD_WIDTH)),
        'conv_lru_w': nrm(ks[17], (DEPTH, CONV_W, LRU_WIDTH), CONV_W ** -0.5),
        'conv_lru_b': nrm(ks[18], (DEPTH, LRU_WIDTH), 0.02),
        'w_rgate': nrm(ks[19], (DEPTH, LRU_BLOCKS, LRU_BLOCK_DIM, LRU_BLOCK_DIM), LRU_BLOCK_DIM ** -0.5),
        'b_rgate': nrm(ks[20], (DEPTH, LRU_WIDTH), 0.02),
        'w_igate': nrm(ks[21], (DEPTH, LRU_BLOCKS, LRU_BLOCK_DIM, LRU_BLOCK_DIM), LRU_BLOCK_DIM ** -0.5),
        'b_igate': nrm(ks[22], (DEPTH, LRU_WIDTH), 0.02),
        'lru_lambda': lru_lambda,
        'norm_lru': gain(ks[23], (DEPTH, LRU_WIDTH)),
        'w_out': nrm(ks[24], (DEPTH, MIX_WIDTH, D_MODEL), MIX_WIDTH ** -0.5),
        'norm_ffn': gain(ks[25], (DEPTH, D_MODEL)),
        'peer_wq': nrm(ks[26], (DEPTH, D_MODEL, PEER_HEADS * PEER_QDIM), D_MODEL ** -0.5),
        'peer_keys': nrm(ks[27], (DEPTH, PEER_HEADS, 2, PEER_KEYS, PEER_HALF), PEER_HALF ** -0.5),
        'peer_u': nrm(ks[28], (DEPTH, PEER_EXPERTS, D_MODEL), D_MODEL ** -0.5),
        'peer_v': nrm(ks[29], (DEPTH, PEER_EXPERTS, D_MODEL), PEER_HEADS ** -0.5),
        'norm_ple_gate': gain(ks[30], (DEPTH, D_MODEL)),
        'w_ple_gate': nrm(ks[31], (DEPTH, D_MODEL, D_MODEL), D_MODEL ** -0.5),
        'w_ple_proj': nrm(ks[32], (DEPTH, PLE_DIM, D_MODEL), PLE_DIM ** -0.5),
        'norm_ple_out': gain(ks[33], (DEPTH, D_MODEL)),
        'norm_final': gain(ks[34], (D_MODEL,)),
    }

def reference(x_prompt, x_sample, state_ssd, state_ssd_conv, state_lru, state_lru_conv,
              p_prompt, p_sample, norm_mix, w_in, conv_ssd_w, conv_ssd_b, dt_bias, a_log,
              d_skip, norm_ssd, conv_lru_w, conv_lru_b, w_rgate, b_rgate, w_igate, b_igate,
              lru_lambda, norm_lru, w_out, norm_ffn, peer_wq, peer_keys, peer_u, peer_v,
              norm_ple_gate, w_ple_gate, w_ple_proj, norm_ple_out, norm_final):
    hp, hs = x_prompt, x_sample
    dt_ = x_prompt.dtype
    sp_ssd, sp_sconv, sp_lru, sp_lconv = [], [], [], []
    ss_ssd, ss_sconv, ss_lru, ss_lconv = [], [], [], []
    for i in range(DEPTH):
        lw = {
            'norm_mix': norm_mix[i], 'w_in': w_in[i],
            'conv_ssd_w': conv_ssd_w[i], 'conv_ssd_b': conv_ssd_b[i],
            'dt_bias': dt_bias[i], 'a_log': a_log[i], 'd_skip': d_skip[i], 'norm_ssd': norm_ssd[i],
            'conv_lru_w': conv_lru_w[i], 'conv_lru_b': conv_lru_b[i],
            'w_rgate': w_rgate[i], 'b_rgate': b_rgate[i], 'w_igate': w_igate[i], 'b_igate': b_igate[i],
            'lru_lambda': lru_lambda[i], 'norm_lru': norm_lru[i], 'w_out': w_out[i],
            'norm_ffn': norm_ffn[i], 'peer_wq': peer_wq[i], 'peer_keys': peer_keys[i],
            'peer_u': peer_u[i], 'peer_v': peer_v[i],
            'norm_ple_gate': norm_ple_gate[i], 'w_ple_gate': w_ple_gate[i],
            'w_ple_proj': w_ple_proj[i], 'norm_ple_out': norm_ple_out[i],
        }
        bp = hp.shape[0]
        hp, a1, a2, a3, a4 = layer(
            hp, p_prompt[i],
            jnp.zeros((bp, SSD_HEADS, SSD_HEAD_DIM, SSD_STATE), dt_),
            jnp.zeros((bp, CONV_W - 1, SSD_CONV_DIM), dt_),
            jnp.zeros((bp, LRU_WIDTH), dt_),
            jnp.zeros((bp, CONV_W - 1, LRU_WIDTH), dt_),
            lw)
        sp_ssd.append(a1); sp_sconv.append(a2); sp_lru.append(a3); sp_lconv.append(a4)
        hs, b1, b2, b3, b4 = layer(hs, p_sample[i], state_ssd[i], state_ssd_conv[i],
                                   state_lru[i], state_lru_conv[i], lw)
        ss_ssd.append(b1); ss_sconv.append(b2); ss_lru.append(b3); ss_lconv.append(b4)
    y_prompt = rmsnorm(hp, norm_final)
    y_sample = rmsnorm(hs, norm_final)
    ssd_state_p = jnp.stack(sp_ssd)
    ssd_conv_p = jnp.stack(sp_sconv)
    lru_state_p = jnp.stack(sp_lru)
    lru_conv_p = jnp.stack(sp_lconv)
    ssd_state_s = jnp.stack(ss_ssd)
    ssd_conv_s = jnp.stack(ss_sconv)
    lru_state_s = jnp.stack(ss_lru)
    lru_conv_s = jnp.stack(ss_lconv)
    return (y_prompt, y_sample, ssd_state_p, ssd_conv_p, lru_state_p, lru_conv_p,
            ssd_state_s, ssd_conv_s, lru_state_s, lru_conv_s)


_drawn_inputs = setup_inputs


def setup_inputs(seed=0):
    import zlib

    import numpy as np

    out = dict(_drawn_inputs(seed))
    spreads = {}
    factors = {'d_skip': 30.441,
     'norm_ssd': 11.352,
     'b_rgate': 8.0,
     'b_igate': 7.396,
     'norm_lru': 11.089,
     'norm_ffn': 10.41,
     'norm_ple_gate': 26.217,
     'norm_ple_out': 18.374,
     'norm_final': 8.122}
    for name, (base, spread) in spreads.items():
        noise = np.random.default_rng([zlib.crc32(name.encode()), seed]).standard_normal(out[name].shape)
        drawn = base * np.exp(spread * noise) if base else spread * noise
        out[name] = __import__('jax').numpy.asarray(drawn.astype(out[name].dtype))
    for name, factor in factors.items():
        out[name] = (out[name] * factor).astype(out[name].dtype)
    return out
```

```python
import concourse.bass as bass
from concourse import mybir
from contextlib import ExitStack

F32 = mybir.dt.float32
F32R = mybir.dt.float32r
BF16 = mybir.dt.bfloat16
U32 = mybir.dt.uint32
ALU = mybir.AluOpType
ACT = mybir.ActivationFunctionType
AX = mybir.AxisListType
ds = bass.ds

P = 128
D = 1024
ND = D // P
NP = 512
NB, LB = 8, 4
T = NP + NB * LB
HT = T // 2
CW = 4
NH, HD, NS, NG = 16, 64, 64, 2
HG = NH // NG
NC = NP // P
NXS = (D + 2 * NG * NS) // P
NXC = NXS + ND
PADP = CW - 1 + NP
PADT = PADP + NB * (CW - 1 + LB)
NCV = PADT - (CW - 1)
EPS = 1e-6
PH, PK, TK = 8, 128, 16
SP_T = P
DT = T - SP_T
NBK = 5
GB = 4
GT_ = DT // GB
GR = 4
NGR = PK // GR
IDS = PH * TK
MIX_TILES = NXC + 3 * ND
KP = 256 // P
NEG = -1e30

COLS = {}
_at = 0
for _name, _n in [("norm_mix", ND), ("conv_w", CW * NXC), ("conv_b", NXC), ("norm_ssd", ND), ("b_r", ND),
                  ("b_i", ND), ("lam", ND), ("norm_lru", ND), ("norm_ffn", ND), ("norm_plg", ND),
                  ("norm_plo", ND), ("norm_fin", ND), ("d_skip", ND)]:
    COLS[_name] = _at
    _at += _n
NCOL = _at


def halves(ap):
    return ap.rearrange("p (h n) -> p h n", h=2)



def plan(nc, start, *specs):
    r = []
    for name, shape, dt in specs:
        n = 4
        for s in shape[1:]:
            n *= s
        assert start + n <= nc.sbuf_usable_end, (name, start, n)
        r.append(nc.alloc_sbuf_tensor_at(name, shape, dt, offset=start))
        start += (n + 31) // 32 * 32
    return r, start


class Shared:

    def __init__(self, nc, ctx):
        self.nc, self.ctx, self.named = nc, ctx, {}
        base = (nc.sbuf_base + 63) // 64 * 64
        (self.h, self.ident, self.ones, self.par, self.epsc), self.free = plan(
            nc, base, ("h", [P, ND, T], F32), ("ident", [P, P], F32), ("ones", [P, P], F32),
            ("par", [P, NCOL], F32), ("epsc", [P, 1], F32))
        self.free = (self.free + 63) // 64 * 64
        self.PS = ctx.enter_context(nc.psum_tensor("PS", [P, 8, 512], F32))

    def sem(self, name):
        if name not in self.named:
            self.named[name] = self.ctx.enter_context(self.nc.semaphore(name))
        return self.named[name]

    def pair(self, s, m=P):
        return self.PS[0:m, 2 * s:2 * s + 2, 0:HT]

    def col(self, name, i, n=1):
        c = COLS[name]
        return self.par[:, c + i:c + i + n]

    def norm_act(self, a, r, src, sq, rstd, ready=None, more=0):
        S = self.sem
        for k in range(ND):
            if r * ND + k >= 2:
                a.wait_ge(S("sq_free"), r * ND + k - 1)
            if ready:
                a.wait_ge(S(ready), more + k + 1)
            a.activation(sq[:, k % 2, :], src[:, k, :], ACT.Square).then_inc(S("sq_ready"), 1)
        a.wait_ge(S("sq_free"), (r + 1) * ND)
        if r >= 1:
            a.wait_ge(S("normed"), r * ND)
        a.activation(halves(rstd[:, :]), self.pair(3), ACT.Sqrt, scale=1.0 / D, bias=self.epsc[:, 0:1]
                     ).then_inc(S("root"), 1)

    def norm_pe(self, pe, r, sq):
        S = self.sem
        for k in range(ND):
            pe.wait_ge(S("sq_ready"), r * ND + k + 1)
            for q in range(2):
                m = pe.matmul(self.pair(3)[:, q, :], self.ones[:, :], sq[:, k % 2, q * HT:(q + 1) * HT],
                              start=(k == 0), stop=(k == ND - 1))
            m.then_inc(S("sq_free"), 1)

    def norm_dve(self, v, r, src, dst, g, rstd):
        S = self.sem
        v.wait_ge(S("root"), r + 1)
        v.reciprocal(rstd[:, :], rstd[:, :]).then_inc(S("rst"), 1)
        v.wait_ge(S("rst"), r + 1)
        for k in range(ND):
            v.scalar_tensor_tensor(out=dst[:, k, :], in0=src[:, k, :], scalar=self.col(g, k), in1=rstd[:, :],
                                   op0=ALU.mult, op1=ALU.mult).then_inc(S("normed"), 1)


def mixer(nc, sh, x, w_xc, w_z, w_gate, w_dt, par, head, w_rg, w_ig, conv_in, s0, lru0, w_out,
          ssd_p, ssd_s, conv_o, lru_o):
    S, PS, pair, col = sh.sem, sh.PS, sh.pair, sh.col
    h, ident, ones, epsc, par_sb = sh.h, sh.ident, sh.ones, sh.epsc, sh.par
    DTV = 27
    LRU_SCAN = 2 * ND + 4

    def at(name, offset, shape, dt=F32):
        return nc.alloc_sbuf_tensor_at(name, shape, dt, offset=offset)

    top = nc.sbuf_usable_end


    o = sh.free
    SL = ND * T * 4

    def take(n):
        nonlocal o
        r = o
        o += (n + 63) // 64 * 64
        return r

    RB, RC, RD, RE, RF = take(SL), take(NXS * T * 4), take(SL), take(SL), take(SL)
    RG = take(2 * 16 * P * 4)
    M1, M2, M3 = take(5 * 1152 * 4), take(SL), take(SL)
    M4 = take(2 * 576 * 4 + 2 * 576 * 4 + T * 4)
    M6 = take(NXC * 24 * 4 + 1952 + ND * 16 * 4)
    M5 = take(12224)
    assert o <= top, (o, top)
    xn = at("xn", RB, [P, ND, T])
    xs = at("xs", RC, [P, NXS, T])
    xl = at("xl", RD, [P, ND, T])
    sz = at("sz", RE, [P, ND, T])
    gg = at("gg", RF, [P, ND, T])
    W = at("w_ring", RG, [P, 2, 16, P])
    xpad = at("xpad", M4, [P, 2, PADT])
    ctmp = at("ctmp", M4 + 2 * 576 * 4, [P, 2, PADT])
    sq = at("sq", M4 + 2 * 576 * 4, [P, 2, T])
    rstd = at("rstd", M4 + 2 * 576 * 4 + 2 * 576 * 4, [P, T])
    cin = at("cin", M6, [P, NXC, NB, CW - 1])
    cout = at("cout", M6 + NXC * 24 * 4, [P, NXC, 27])
    wdt = at("wdt", M6 + 1728 + 1952, [P, ND, NH])
    xhi = at("xhi", M1, [P, ND, T], F32R)
    xlo = at("xlo", RB, [P, ND, T], F32R)
    Whi = at("Whi", M2, [P, 2, ND, P], F32R)
    Wlo = at("Wlo", M2 + 8192, [P, 2, ND, P], F32R)
    rg = at("rg", M1, [P, ND, T])
    ig = at("ig", M2, [P, ND, T])
    av = at("av", M3, [P, ND, T])
    th = at("th", RB, [P, ND, T])
    wr = at("wr", RG, [P, ND, P])
    wi = at("wi", RG + 4096, [P, ND, P])
    ce = at("ce", RB, [P, HG, T])
    xtm = at("xtm", M1, [P, NC + 1, 1152])
    s0s = at("s0s", M2, [P, HG, NB, HD])
    L = at("L", M3, [P, NH, P])
    SC = at("SC", M3 + 8192, [P, NH, P])
    dtw = at("dtw", M3, [NH, 6, T])
    smask = at("smask", M3 + 6 * T * 4, [NH, T])
    Bw = at("Bw", M4, [P, NH, NS])
    XM = at("XM", M4 + 4096, [32, 2, NB, HD])
    ys = at("ys", RF, [P, ND, T])
    selG = at("selG", RG + 8192, [NH, HG, P])
    cz = [at("cz0", RG + 12288, [P, T]), at("cz1", M4 + 8192, [P, T])]
    selH = at("selH", RG, [NH, NH, P])
    q5 = M5
    def t5(name, shape):
        nonlocal q5
        n = 4
        for s in shape[1:]:
            n *= s
        r = at(name, q5, shape)
        q5 += (n + 31) // 32 * 32
        assert q5 <= M5 + 12224
        return r
    dts = t5("dts", [NH, T])
    acs = t5("acs", [NH, T])
    ST = t5("ST", [P, HG * HD])
    CB = t5("CB", [P, NG, P])
    negm = t5("negm", [P, P])
    negs = t5("negs", [32, 32])
    sell = t5("sell", [P, P])
    sel4 = t5("sel4", [P, P])
    seg = t5("seg", [32, NB])
    acm = t5("acm", [P, NC + 1, NH])
    nacm = t5("nacm", [P, NC + 1, NH])
    dtm = t5("dtm", [P, NC + 1, NH])
    wtm = t5("wtm", [P, NC + 1, NH])
    dec = t5("dec", [P, HG, NC + NB])
    hv = t5("hv", [NH, 4])
    lv = t5("lv", [P, 7, ND])
    spl = t5("spl", [P, 2, ND])
    l0 = t5("l0", [P, ND, NB])
    lt = t5("lt", [P, ND, NB])
    lo = t5("lo", [P, ND, 1 + NB])


    XC0, Z0, G0, O0 = 0, NXC, NXC + ND, NXC + 2 * ND

    def load_w(sp, n0, count, src, K):
        with sp.Fori(0, count // 2) as i:
            for s in range(2):
                if n0:
                    sp.wait_ge(S("mm") if n0 == O0 else S("wlo"), i * 2 + (n0 - 1 + s))
                sp.dma_start(W[:, s, 0:K, :], src[ds(i * 2 + s, 1), :, :, :].rearrange("a p k m -> p (a k) m")
                             ).then_inc(S("wf0" if s == 0 else "wf1"), 16)

    def project(pe, n0, count):
        with pe.Fori(0, count // 2) as i:
            for s in range(2):
                pe.wait_ge(S("wlo"), i * 2 + (n0 + s + 1))
                pe.wait_ge(S("pf0" if s == 0 else "pf1"), i + (n0 // 2 + 1))
                for k in range(ND):
                    for w_sb, x_sb, first, last in ((Whi, xhi, k == 0, False), (Whi, xlo, False, False),
                                                    (Wlo, xhi, False, k == ND - 1)):
                        for q in range(2):
                            m = pe.matmul(pair(s)[:, q, :], w_sb[:, s, k, :], x_sb[:, k, q * HT:(q + 1) * HT],
                                          start=first, stop=last)
                m.then_inc(S("mm"), 1)

    def split_hi(a, i, s, n0):
        n = s + n0
        at_ = lambda k, by: k if i is None else i * by + k
        a.wait_ge(S("wf%d" % s), at_(16 * (n // 2 + 1), 16))
        if i is not None or n >= 2:
            a.wait_ge(S("mm"), at_(n - 1, 2))
        a.copy(Whi[:, s, :, :], W[:, s, 0:ND, :]).then_inc(S("whi"), 1)

    def split_lo(v, i, s, n0):
        n = s + n0
        v.wait_ge(S("whi"), n + 1 if i is None else i * 2 + (n + 1))
        v.tensor_tensor(Wlo[:, s, :, :], W[:, s, 0:ND, :], Whi[:, s, :, :].bitcast(F32), ALU.subtract
                        ).then_inc(S("wlo"), 1)

    def cval(s):
        return ctmp[:, s, PADP:PADT].rearrange("p (b t) -> p b t", b=NB)[:, :, 0:LB]


    def sync(sp):
        sp.dma_start(h[:, :, :], x).then_inc(S("x_in"), 16)
        sp.dma_start(par_sb[:, :], par).then_inc(S("par_in"), 16)
        sp.dma_start(cin[:, :, :, :], conv_in).then_inc(S("conv_in_s"), 16)
        sp.dma_start(wdt[:, :, :], w_dt).then_inc(S("wdt_in"), 16)
        sp.dma_start(hv[:, 0:2], head).then_inc(S("small_in"), 16)
        sp.dma_start(l0[:, :, :], lru0).then_inc(S("small_in"), 16)
        for s in range(2):
            sp.dma_start(W[:, s, 0:ND, :], w_xc[s, :, :, :]).then_inc(S("wf0" if s == 0 else "wf1"), 16)
        with sp.Fori(0, NXC // 2 - 1) as i:
            for s in range(2):
                sp.wait_ge(S("wlo"), i * 2 + (s + 1))
                sp.dma_start(W[:, s, 0:ND, :],
                             w_xc[ds(i * 2 + (s + 2), 1), :, :, :].rearrange("a p k m -> p (a k) m")
                             ).then_inc(S("wf0" if s == 0 else "wf1"), 16)
        load_w(sp, Z0, ND, w_z, ND)
        load_w(sp, G0, ND, w_gate, ND)
        sp.wait_ge(S("lw_zero"), 2)
        for w_sb, w_in in ((wr, w_rg), (wi, w_ig)):
            for q in range(2):
                sp.dma_start(w_sb[q * 64:q * 64 + 64, :, q * 64:q * 64 + 64],
                             w_in[:, q, :, :].rearrange("m i j -> i m j")).then_inc(S("lw_in"), 16)
        sp.wait_ge(S("cout_s"), NXC)
        sp.dma_start(conv_o, cout[:, :, :]).then_inc(S("out_s"), 16)
        sp.wait_ge(S("lru"), LRU_SCAN)
        sp.dma_start(s0s[:, :, :, :], s0).then_inc(S("s0_in"), 16)
        sp.wait_ge(S("lru"), LRU_SCAN + 2)
        sp.dma_start(lru_o, lo[:, :, :]).then_inc(S("out_s"), 16)
        sp.wait_ge(S("stu"), 2 * NC)
        sp.dma_start(ssd_p, ST[:, :]).then_inc(S("out_s"), 16)
        sp.wait_ge(S("st_s"), 2 * HG)
        sp.dma_start(ssd_s, s0s[:, :, :, :]).then_inc(S("out_s"), 16)
        load_w(sp, O0, ND, w_out, 16)
        sp.wait_ge(S("pf0"), (O0 + ND) // 2 + 1)
        sp.wait_ge(S("pf1"), (O0 + ND) // 2 + 1)

    def pool(g):
        g.memset(ident[:, :], 0.0).then_inc(S("const"), 1)
        g.memset(ones[:, :], 1.0).then_inc(S("const"), 1)
        g.memset(negm[:, :], 0.0).then_inc(S("const"), 1)
        g.memset(negs[:, :], 0.0).then_inc(S("const"), 1)
        g.memset(sell[:, :], 0.0).then_inc(S("const"), 1)
        g.memset(sel4[:, :], 0.0).then_inc(S("const"), 1)
        g.memset(seg[:, :], 1.0).then_inc(S("const"), 1)
        g.memset(epsc[:, :], EPS).then_inc(S("const"), 1)
        g.memset(xpad[:, :, :], 0.0).then_inc(S("const"), 1)
        g.memset(acm[:, :, :], 0.0).then_inc(S("const"), 1)
        g.memset(dtm[:, :, :], 0.0).then_inc(S("const"), 1)
        g.wait_ge(S("const"), 11)
        g.affine_select(out=ident[:, :], in_=ident[:, :], compare_op=ALU.not_equal, fill=1.0, base=0,
                        pattern=[[-1, P]], channel_multiplier=1).then_inc(S("const"), 1)
        g.affine_select(out=negm[:, :], in_=negm[:, :], compare_op=ALU.is_ge, fill=NEG, base=0,
                        pattern=[[1, P]], channel_multiplier=-1).then_inc(S("const"), 1)
        g.affine_select(out=negs[:, :], in_=negs[:, :], compare_op=ALU.is_ge, fill=NEG, base=0,
                        pattern=[[1, 32]], channel_multiplier=-1).then_inc(S("const"), 1)
        g.wait_ge(S("const"), 14)
        g.affine_select(out=negs[:, :], in_=negs[:, :], compare_op=ALU.is_ge, fill=NEG, base=0,
                        pattern=[[-LB, NB], [0, LB]], channel_multiplier=1).then_inc(S("const"), 1)
        g.affine_select(out=sell[:, :], in_=sell[:, :], compare_op=ALU.not_equal, fill=1.0, base=-(P - 1),
                        pattern=[[0, P]], channel_multiplier=1).then_inc(S("const"), 1)
        g.affine_select(out=sel4[:, :], in_=sel4[:, :], compare_op=ALU.not_equal, fill=1.0, base=-(LB - 1),
                        pattern=[[-LB, P // LB], [0, LB]], channel_multiplier=1).then_inc(S("const"), 1)
        g.affine_select(out=seg[:, :], in_=seg[:, :], compare_op=ALU.is_ge, fill=0.0, base=0,
                        pattern=[[-LB, NB]], channel_multiplier=1).then_inc(S("const"), 1)
        g.wait_ge(S("const"), 18)
        g.affine_select(out=seg[:, :], in_=seg[:, :], compare_op=ALU.is_ge, fill=0.0, base=LB - 1,
                        pattern=[[LB, NB]], channel_multiplier=-1).then_inc(S("const"), 1)
        g.wait_ge(S("conv_in_s"), 16)
        with g.Fori(0, NXC // 2) as i:
            for s in range(2):
                g.wait_ge(S("cv"), i * 8 + 4 * (s + 1))
                g.tensor_copy(xpad[:, s, PADP:PADT].rearrange("p (b t) -> p b t", b=NB)[:, :, 0:CW - 1],
                              cin[:, ds(i * 2 + s, 1), :, :].rearrange("p a b t -> p (a b) t")
                              ).then_inc(S("pad_prep"), 1)
            for s in range(2):
                g.wait_ge(S("evac"), i * 6 + 3 * (s + 1))
                g.tensor_copy(cout[:, ds(i * 2 + s, 1), 0:3], xpad[:, s:s + 1, NP:PADP]
                              ).then_inc(S("pad_free"), 1)
                g.tensor_copy(cout[:, ds(i * 2 + s, 1), 3:27].rearrange("p a (b t) -> p (a b) t", b=NB),
                              xpad[:, s, PADP:PADT].rearrange("p (b t) -> p b t", b=NB)[:, :, LB:LB + CW - 1]
                              ).then_inc(S("cout_s"), 1)
        g.wait_ge(S("mm"), O0)
        g.memset(wr[:, :, :], 0.0).then_inc(S("lw_zero"), 1)
        g.memset(wi[:, :, :], 0.0).then_inc(S("lw_zero"), 1)
        g.wait_ge(S("rg_mm"), ND)
        g.memset(selG[:, :, :], 0.0).then_inc(S("sel_c"), 1)
        g.memset(selH[:, :, :], 0.0).then_inc(S("sel_c"), 1)
        g.wait_ge(S("sel_c"), 2)
        g.affine_select(out=selG[:, :, :].rearrange("k h (a m) -> k h a m", a=2),
                        in_=selG[:, :, :].rearrange("k h (a m) -> k h a m", a=2),
                        compare_op=ALU.not_equal, fill=1.0, base=0,
                        pattern=[[-1, HG], [-HG, NG], [0, NS]], channel_multiplier=1).then_inc(S("sel_c"), 1)
        g.affine_select(out=selH[:, :, :], in_=selH[:, :, :], compare_op=ALU.not_equal, fill=1.0, base=0,
                        pattern=[[-1, NH], [0, P]], channel_multiplier=1).then_inc(S("sel_c"), 1)

    def tensor(pe):
        pe.wait_ge(S("const"), 19)
        sh.norm_pe(pe, 0, sq)
        pe.wait_ge(S("normed"), ND)
        pe.wait_ge(S("wdt_in"), 16)
        for k in range(ND):
            for q in range(2):
                m = pe.matmul(PS[0:NH, 4 + q, 0:HT], wdt[:, k, :], xn[:, k, q * HT:(q + 1) * HT],
                              start=(k == 0), stop=(k == ND - 1))
        m.then_inc(S("dtp"), 1)
        pe.wait_ge(S("xlo"), ND)
        project(pe, XC0, NXC)
        project(pe, Z0, ND)
        project(pe, G0, ND)
        pe.wait_ge(S("lw_in"), 64)
        pe.wait_ge(S("act_c"), 4 + 2 * NXC)
        pe.wait_ge(S("pf0"), O0 // 2 + 1)
        pe.wait_ge(S("pf1"), O0 // 2 + 1)
        for m_ in range(ND):
            if m_ >= 2:
                pe.wait_ge(S("sig"), 2 * (m_ - 1))
            for w_sb, bank in ((wr, 0), (wi, 1)):
                for q in range(2):
                    mm_ = pe.matmul(pair(2 * (m_ % 2) + bank)[:, q, :], w_sb[:, m_, :], xl[:, m_, q * HT:(q + 1) * HT],
                                    start=True, stop=True)
            mm_.then_inc(S("rg_mm"), 1)
        pe.wait_ge(S("spv"), DTV)
        pe.wait_ge(S("sig"), 2 * ND)
        n = 0
        for src in (acs, dts):
            for c in range(NC + 1):
                w = P if c < NC else 32
                m = pe.transpose(PS[0:w, 4, n * NH:(n + 1) * NH], src[:, c * P:c * P + w], ident[0:NH, 0:NH])
                n += 1
        m.then_inc(S("wts_p"), 1)
        pe.wait_ge(S("wts_v"), 2)
        for c in range(NC + 1):
            m = pe.matmul(PS[:, 5, c * NH:(c + 1) * NH], (sell if c < NC else sel4)[:, :], acm[:, c, :],
                          start=True, stop=True)
        m.then_inc(S("wts_p"), 1)
        n = 0
        for c in range(NC + 1):
            w = P if c < NC else 32
            for f in range(0, 9, 3):
                if n >= 4:
                    pe.wait_ge(S("trc"), n - 3)
                for t in range(f, f + 3):
                    m = pe.transpose(PS[0:w, n % 4, (t - f) * P:(t - f + 1) * P], xs[:, t, c * P:c * P + w],
                                     ident[:, :])
                m.then_inc(S("tr"), 1)
                n += 1
        pe.wait_ge(S("sel_c"), 4)
        pe.wait_ge(S("wts_v"), 4)
        pe.wait_ge(S("trc"), 15)
        for j in range(HG):
            if j >= 2:
                pe.wait_ge(S("rowe"), j - 1)
            for q in range(2):
                m = pe.matmul(pair(j % 2)[:, q, :], selG[:, j, :], acs[:, q * HT:(q + 1) * HT],
                              start=True, stop=True)
            m.then_inc(S("row"), 1)
        pe.wait_ge(S("rowe"), HG)
        pe.wait_ge(S("czd"), 2 * NG)
        for c in range(NC + 1):
            w = P if c < NC else 32
            sl = slice(c * P, c * P + w)
            if c >= 1:
                pe.wait_ge(S("cbc"), c)
            for g in range(NG):
                m = pe.matmul(PS[0:w, 4, g * P:g * P + w], xs[:, 8, sl],
                              cz[g][:, sl], start=True, stop=True)
            m.then_inc(S("cb"), 1)
            if c >= 1:
                pe.wait_ge(S("lexp"), NH * c)
            for hd in range(NH):
                b, f = hd // 4, hd % 4
                pe.matmul(PS[0:w, b, f * P:f * P + w], selH[:, hd, 0:w], acs[:, sl], start=True, stop=False)
                m = pe.matmul(PS[0:w, b, f * P:f * P + w], ident[0:w, 0:w],
                              (negm if c < NC else negs)[:, :], start=False, stop=True)
                if f == 3:
                    m.then_inc(S("bc"), 1)
            if c >= 1:
                pe.wait_ge(S("yad"), 2 * c)
            if c == 0:
                pe.wait_ge(S("cem"), 1)
            if c == NC:
                pe.wait_ge(S("s0_in"), 16)
            for hd in range(NH):
                g, j = hd // HG, hd % HG
                m_, q = hd // 2, hd % 2
                pe.wait_ge(S("scs"), NH * c + hd + 1)
                out = PS[q * 64:q * 64 + 64, 5 + m_ // 4, (m_ % 4) * P:(m_ % 4) * P + w]
                m = pe.matmul(out, xtm[0:w, c, hd * HD:(hd + 1) * HD], SC[0:w, hd, 0:w], start=True,
                              stop=(c == 0 or c == NC))
                if 0 < c < NC:
                    if hd == 0:
                        pe.wait_ge(S("stu"), 2 * c)
                    m = pe.matmul(out, ST[g * 64:g * 64 + 64, j * HD:(j + 1) * HD],
                                  ce[g * 64:g * 64 + 64, j, sl], start=False, stop=True)
                if c == NC:
                    for b in range(NB):
                        m = pe.matmul(PS[q * 64:q * 64 + 64, 5 + m_ // 4, (m_ % 4) * P + b * LB:(m_ % 4) * P + b * LB + LB],
                                      s0s[g * 64:g * 64 + 64, j, b, :],
                                      ce[g * 64:g * 64 + 64, j, NP + b * LB:NP + (b + 1) * LB],
                                      start=False, stop=True, skip_group_check=True)
                if hd % 8 == 7:
                    m.then_inc(S("ymm"), 1)
            if c < NC:
                pe.wait_ge(S("bwd"), c + 1)
                for hd in range(NH):
                    g, j = hd // HG, hd % HG
                    m = pe.matmul(PS[g * 64:g * 64 + 64, 7, j * HD:(j + 1) * HD], Bw[:, hd, :],
                                  xtm[:, c, hd * HD:(hd + 1) * HD], start=True, stop=True)
                m.then_inc(S("stm"), 1)
        pe.wait_ge(S("bwd"), NC + 1)
        pe.wait_ge(S("lexp"), NH * (NC + 1))
        for j in range(HG):
            if j >= 2:
                pe.wait_ge(S("st_s"), 2 * (j - 1))
            for g in range(NG):
                pe.wait_ge(S("xmd"), 2 * j + g + 1)
                m = pe.matmul(PS[g * 64:g * 64 + 64, j % 2, :], Bw[0:32, g * HG + j, :],
                              XM[:, g, :, :].rearrange("l b p -> l (b p)"), start=True, stop=True)
                if g == 0:
                    m.then_inc(S("stm"), 1)
            m.then_inc(S("stm"), 1)
        sh.norm_pe(pe, 1, sq)
        sh.norm_pe(pe, 2, sq)
        pe.wait_ge(S("normed"), 3 * ND)
        pe.wait_ge(S("st_s"), 2 * HG)
        with pe.Fori(0, ND // 2) as i:
            for s in range(2):
                pe.wait_ge(S("wf0" if s == 0 else "wf1"), i * 16 + 16 * (O0 // 2 + 1))
                pe.wait_ge(S("pf0" if s == 0 else "pf1"), i + (O0 // 2 + 1))
                for k in range(16):
                    src = ys if k < ND else xl
                    for q in range(2):
                        m = pe.matmul(pair(s)[:, q, :], W[:, s, k, :], src[:, k % ND, q * HT:(q + 1) * HT],
                                      start=(k == 0), stop=(k == 15))
                m.then_inc(S("mm"), 1)

    def scalar(a):
        a.sem_inc(S("act_c"), 4)
        a.wait_ge(S("x_in"), 16)
        a.wait_ge(S("const"), 19)
        sh.norm_act(a, 0, h, sq, rstd)
        for s in range(2):
            split_hi(a, None, s, 0)
        for k in range(ND):
            a.wait_ge(S("normed"), k + 1)
            a.copy(xhi[:, k, :], xn[:, k, :]).then_inc(S("xhi"), 1)

        def compact(func, count, n0, dst):
            with a.Fori(0, count // 2) as i:
                for s in range(2):
                    split_hi(a, i, s, n0 + 2)
                    a.wait_ge(S("cv"), i * 8 + (4 * (n0 + s + 1) + 8))
                    a.activation(dst[:, ds(i * 2 + s, 1), 0:NP], ctmp[:, s:s + 1, 0:NP], func
                                 ).then_inc(S("act_c"), 1)
                    a.activation(dst[:, ds(i * 2 + s, 1), NP:T].rearrange("p a (b t) -> p (a b) t", b=NB),
                                 cval(s), func).then_inc(S("act_c"), 1)

        def gated(func, n0, dst):
            with a.Fori(0, ND // 2 - (n0 == G0)) as i:
                for s in range(2):
                    split_hi(a, i, s, n0 + 2)
                    a.wait_ge(S("mm"), i * 2 + (n0 + s + 1))
                    a.activation(dst[:, ds(i * 2 + s, 1), :].rearrange("p a (h n) -> p (a h) n", h=2), pair(s),
                                 func).then_inc(S("pf0" if s == 0 else "pf1"), 1)
            if n0 == G0:
                for s in range(2):
                    a.wait_ge(S("mm"), n0 + ND - 1 + s)
                    a.activation(halves(dst[:, ND - 2 + s, :]), pair(s), func).then_inc(S("pf%d" % s), 1)

        a.preload_act_table(ACT.Silu)
        compact(ACT.Silu, NXS, 0, xs)
        compact(ACT.Copy, ND, NXS, xl)
        gated(ACT.Silu, Z0, sz)
        a.preload_act_table(ACT.Gelu_apprx_tanh)
        gated(ACT.Gelu_apprx_tanh, G0, gg)
        for m_ in range(ND):
            a.wait_ge(S("rg_mm"), m_ + 1)
            a.activation(halves(rg[:, m_, :]), pair(2 * (m_ % 2)), ACT.Sigmoid, bias=col("b_r", m_)).then_inc(S("sig"), 1)
            a.activation(halves(ig[:, m_, :]), pair(2 * (m_ % 2) + 1), ACT.Sigmoid, bias=col("b_i", m_)).then_inc(S("sig"), 1)
        a.activation(lv[:, 0, :], col("lam", 0, ND), ACT.Abs).then_inc(S("spa"), 1)
        a.wait_ge(S("spa"), 1)
        a.activation(lv[:, 0, :], lv[:, 0, :], ACT.Exp, scale=-1.0).then_inc(S("spa"), 1)
        a.wait_ge(S("spv"), 2)
        a.activation(lv[:, 2, :], lv[:, 1, :], ACT.Ln).then_inc(S("spa"), 1)
        a.wait_ge(S("spv"), 12)
        a.wait_ge(S("sig"), 2 * ND)
        a.preload_act_table(ACT.Tanh)
        for m_ in range(ND):
            a.activation(av[:, m_, :], rg[:, m_, :], ACT.Exp, scale=spl[:, 0, m_:m_ + 1]).then_inc(S("ltab"), 1)
            a.activation(th[:, m_, :], rg[:, m_, :], ACT.Tanh, scale=spl[:, 1, m_:m_ + 1]).then_inc(S("ltab"), 1)
        for m_ in range(ND):
            a.wait_ge(S("l1ma"), 2 * (m_ + 1))
            a.activation(th[:, m_, :], th[:, m_, :], ACT.Sqrt).then_inc(S("lroot"), 1)
        a.wait_ge(S("lru"), LRU_SCAN)
        a.activation(dtw[:, 0, :], dts[:, :], ACT.Abs).then_inc(S("spa"), 1)
        a.wait_ge(S("spa"), 4)
        a.activation(dtw[:, 0, :], dtw[:, 0, :], ACT.Exp, scale=-1.0).then_inc(S("spa"), 1)
        a.activation(hv[:, 2:3], hv[:, 1:2], ACT.Exp).then_inc(S("spa"), 1)
        a.wait_ge(S("spv"), 14)
        a.activation(dtw[:, 2, :], dtw[:, 1, :], ACT.Ln).then_inc(S("spa"), 1)
        a.wait_ge(S("wts_v"), 6)
        a.activation(wtm[:, :, :], wtm[:, :, :], ACT.Exp).then_inc(S("wts_a"), 1)
        n = 0
        for c in range(NC + 1):
            w = P if c < NC else 32
            for f in range(0, 9, 3):
                a.wait_ge(S("tr"), n + 1)
                a.copy(xtm[0:w, c, f * P:(f + 3) * P], PS[0:w, n % 4, 0:3 * P]).then_inc(S("trc"), 1)
                n += 1
        for j in range(HG):
            a.wait_ge(S("row"), j + 1)
            a.activation(halves(ce[:, j, :]), pair(j % 2), ACT.Exp).then_inc(S("rowe"), 1)
        for c in range(NC + 1):
            w = P if c < NC else 32
            if c >= 1:
                a.wait_ge(S("scs"), NH * c)
            for hd in range(NH):
                if hd % 4 == 0:
                    a.wait_ge(S("bc"), 4 * c + hd // 4 + 1)
                a.activation(L[0:w, hd, 0:w], PS[0:w, hd // 4, (hd % 4) * P:(hd % 4) * P + w], ACT.Exp,
                             bias=nacm[0:w, c, hd:hd + 1]).then_inc(S("lexp"), 1)
        a.wait_ge(S("ys_done"), 1)
        sh.norm_act(a, 1, ys, sq, rstd)
        sh.norm_act(a, 2, xl, sq, rstd)

    def vector(v):
        v.sem_inc(S("cv"), 8)
        v.sem_inc(S("pf0"), 1)
        v.sem_inc(S("pf1"), 1)
        v.wait_ge(S("par_in"), 16)
        v.wait_ge(S("x_in"), 16)
        sh.norm_dve(v, 0, h, xn, "norm_mix", rstd)
        v.wait_ge(S("small_in"), 32)
        v.wait_ge(S("dtp"), 1)
        v.tensor_scalar(halves(dts[:, :]), PS[0:NH, 4:6, 0:HT], hv[:, 0:1], None, ALU.add
                        ).then_inc(S("dt_v"), 1)
        for s in range(2):
            split_lo(v, None, s, 0)
        for k in range(ND):
            v.wait_ge(S("xhi"), k + 1)
            v.tensor_tensor(xlo[:, k, :], xn[:, k, :], xhi[:, k, :].bitcast(F32), ALU.subtract
                            ).then_inc(S("xlo"), 1)
        with v.Fori(0, NXC // 2) as i:
            for s in range(2):
                v.wait_ge(S("mm"), i * 2 + (s + 1))
                v.wait_ge(S("pad_prep"), i * 2 + (s + 1))
                v.tensor_copy(xpad[:, s, CW - 1:CW - 1 + HT], PS[:, 2 * s, 0:HT]).then_inc(S("evac"), 1)
                v.tensor_copy(xpad[:, s, CW - 1 + HT:PADP], PS[:, 2 * s + 1, 0:NP - HT]).then_inc(S("evac"), 1)
                v.tensor_copy(xpad[:, s, PADP:PADT].rearrange("p (b t) -> p b t", b=NB)[:, :, CW - 1:],
                              PS[:, 2 * s + 1, NP - HT:HT].rearrange("p (b t) -> p b t", b=NB)
                              ).then_inc(S("evac"), 1)
                v.wait_ge(S("evac"), i * 6 + 3 * (s + 1))
                v.sem_inc(S("pf0" if s == 0 else "pf1"), 1)
                v.wait_ge(S("act_c"), i * 4 + 2 * (s + 1))
                wcol = lambda k: par_sb[:, ds(i * 2 + (COLS["conv_w"] + NXC * k + s), 1)]
                v.tensor_scalar(ctmp[:, s, 0:NCV], xpad[:, s, 0:NCV], wcol(0),
                                par_sb[:, ds(i * 2 + (COLS["conv_b"] + s), 1)], ALU.mult, ALU.add
                                ).then_inc(S("cv"), 1)
                for k in range(1, CW):
                    v.wait_ge(S("cv"), i * 8 + (4 * s + k + 8))
                    v.scalar_tensor_tensor(out=ctmp[:, s, 0:NCV], in0=xpad[:, s, k:k + NCV], scalar=wcol(k),
                                           in1=ctmp[:, s, 0:NCV], op0=ALU.mult, op1=ALU.add).then_inc(S("cv"), 1)
                split_lo(v, i, s, XC0 + 2)

        with v.Fori(0, ND - 1) as i:
            for s in range(2):
                split_lo(v, i, s, Z0 + 2)

        def log1p(n0, e, x, b, first):
            w = S("spv")
            v.wait_ge(S("spa"), first)
            v.tensor_scalar(b(1), b(0), 1.0, None, ALU.add).then_inc(w, 1)
            v.wait_ge(w, n0 + 1)
            v.tensor_scalar(b(3), b(1), 1.0, None, ALU.subtract).then_inc(w, 1)
            v.wait_ge(w, n0 + 2)
            v.scalar_tensor_tensor(out=b(4), in0=b(3), scalar=0.0, in1=b(0), op0=ALU.is_equal, op1=ALU.mult
                                   ).then_inc(w, 1)
            v.tensor_scalar(b(5), b(3), 1e-30, None, ALU.max).then_inc(w, 1)
            v.wait_ge(w, n0 + 4)
            v.reciprocal(b(5), b(5)).then_inc(w, 1)
            v.wait_ge(w, n0 + 5)
            v.tensor_tensor(b(5), b(5), b(0), ALU.mult).then_inc(w, 1)
            v.wait_ge(w, n0 + 6)
            v.wait_ge(S("spa"), x)
            v.tensor_tensor(b(5), b(5), b(2), ALU.mult).then_inc(w, 1)
            v.wait_ge(w, n0 + 7)
            v.tensor_tensor(b(5), b(5), b(4), ALU.add).then_inc(w, 1)
            v.wait_ge(w, n0 + 8)

        w = S("spv")
        log1p(0, None, 3, lambda i: lv[:, i, :], 2)
        v.tensor_scalar(lv[:, 6, :], col("lam", 0, ND), -1.0, 0.0, ALU.mult, ALU.max).then_inc(w, 1)
        v.wait_ge(w, 9)
        v.tensor_tensor(lv[:, 5, :], lv[:, 5, :], lv[:, 6, :], ALU.add).then_inc(w, 1)
        v.wait_ge(w, 10)
        v.tensor_scalar(spl[:, 0, :], lv[:, 5, :], -8.0, None, ALU.mult).then_inc(w, 1)
        v.tensor_scalar(spl[:, 1, :], lv[:, 5, :], 8.0, None, ALU.mult).then_inc(w, 1)

        u = S("lru")
        v.wait_ge(S("act_c"), 4 + 2 * NXC)
        v.wait_ge(S("sig"), 2 * ND)
        v.tensor_tensor(ig[:, :, :], ig[:, :, :], xl[:, :, :], ALU.mult).then_inc(u, 1)
        for m_ in range(ND):
            v.wait_ge(S("ltab"), 2 * (m_ + 1))
            v.tensor_tensor(rg[:, m_, :], av[:, m_, :], av[:, m_, :], ALU.mult).then_inc(S("l1ma"), 1)
            v.wait_ge(S("l1ma"), 2 * m_ + 1)
            v.scalar_tensor_tensor(out=th[:, m_, :], in0=rg[:, m_, :], scalar=1.0, in1=th[:, m_, :], op0=ALU.add,
                                   op1=ALU.mult).then_inc(S("l1ma"), 1)
        v.wait_ge(u, 1)
        for m_ in range(ND):
            v.wait_ge(S("lroot"), m_ + 1)
            v.tensor_tensor(ig[:, m_, :], ig[:, m_, :], th[:, m_, :], ALU.mult).then_inc(u, 1)
        v.tensor_tensor(lt[:, :, :], av[:, :, NP:T:LB], l0[:, :, :], ALU.mult).then_inc(u, 1)
        v.wait_ge(u, ND + 2)
        v.tensor_tensor(ig[:, :, NP:T:LB], ig[:, :, NP:T:LB], lt[:, :, :], ALU.add).then_inc(u, 1)
        v.memset(av[:, :, NP:T:LB], 0.0).then_inc(u, 1)
        v.wait_ge(u, ND + 4)
        for m_ in range(ND):
            v.tensor_tensor_scan(out=rg[:, m_, :], data0=av[:, m_, :], data1=ig[:, m_, :], initial=0.0,
                                 op0=ALU.mult, op1=ALU.add).then_inc(u, 1)
        v.wait_ge(u, LRU_SCAN)
        v.tensor_copy(lo[:, :, 0:1], rg[:, :, NP - 1:NP]).then_inc(u, 1)
        v.tensor_copy(lo[:, :, 1:], rg[:, :, NP + LB - 1:T:LB]).then_inc(u, 1)
        v.wait_ge(S("pf1"), G0 // 2 + ND // 2 + 1)
        v.tensor_tensor(xl[:, :, :], rg[:, :, :], gg[:, :, :], ALU.mult).then_inc(u, 1)

        log1p(12, None, 7, lambda i: dtw[:, i, :], 5)
        v.scalar_tensor_tensor(out=dts[:, :], in0=dts[:, :], scalar=0.0, in1=dtw[:, 5, :], op0=ALU.max,
                               op1=ALU.add).then_inc(w, 1)
        v.tensor_scalar(hv[:, 3:4], hv[:, 2:3], -1.0, None, ALU.mult).then_inc(w, 1)
        v.memset(smask[:, :], 1.0).then_inc(w, 1)
        v.wait_ge(w, 23)
        v.memset(smask[:, 0:NP:P], 0.0).then_inc(w, 1)
        v.memset(smask[:, NP:T:LB], 0.0).then_inc(w, 1)
        v.tensor_scalar(dtw[:, 4, :], dts[:, :], hv[:, 3:4], None, ALU.mult).then_inc(w, 1)
        v.wait_ge(w, 26)
        v.tensor_tensor_scan(out=acs[:, :], data0=smask[:, :], data1=dtw[:, 4, :], initial=0.0, op0=ALU.mult,
                             op1=ALU.add).then_inc(w, 1)

        k = S("wts_v")
        v.wait_ge(S("wts_p"), 1)
        n4 = NC * NH
        v.tensor_copy(acm[:, 0:NC, :], PS[:, 4, 0:n4].rearrange("p (c h) -> p c h", h=NH)).then_inc(k, 1)
        v.tensor_copy(acm[0:32, NC, :], PS[0:32, 4, n4:n4 + NH]).then_inc(k, 1)
        v.tensor_copy(dtm[:, 0:NC, :], PS[:, 4, n4 + NH:2 * n4 + NH].rearrange("p (c h) -> p c h", h=NH)
                      ).then_inc(k, 1)
        v.tensor_copy(dtm[0:32, NC, :], PS[0:32, 4, 2 * n4 + NH:2 * n4 + 2 * NH]).then_inc(k, 1)
        v.wait_ge(k, 2)
        v.tensor_scalar(nacm[:, :, :], acm[:, :, :], -1.0, None, ALU.mult).then_inc(k, 1)
        v.wait_ge(S("wts_p"), 2)
        v.tensor_tensor(wtm[:, :, :], PS[:, 5, 0:(NC + 1) * NH].rearrange("p (c h) -> p c h", h=NH),
                        acm[:, :, :], ALU.subtract).then_inc(k, 1)
        v.wait_ge(S("wts_a"), 1)
        v.wait_ge(k, 6)
        v.tensor_tensor(wtm[:, :, :], wtm[:, :, :], dtm[:, :, :], ALU.mult).then_inc(k, 1)
        v.wait_ge(S("trc"), 15)
        for t in range(ND):
            v.tensor_scalar(xs[:, t, :], xs[:, t, :], col("d_skip", t), None, ALU.mult).then_inc(S("xd"), 1)
        v.wait_ge(S("cout_s"), NXC)
        for g in range(NG):
            v.memset(cz[g][64 * (1 - g):64 * (2 - g), :], 0.0).then_inc(S("czd"), 1)
            v.tensor_copy(cz[g][64 * g:64 * g + 64, :], xs[64 * g:64 * g + 64, 9, :]).then_inc(S("czd"), 1)
        v.wait_ge(S("rowe"), HG)
        v.tensor_copy(dec[:, :, 0:NC], ce[:, :, P - 1:NP:P]).then_inc(S("decs"), 1)
        v.tensor_copy(dec[:, :, NC:], ce[:, :, NP + LB - 1:T:LB]).then_inc(S("decs"), 1)
        v.wait_ge(S("decs"), 2)
        v.tensor_tensor(ce[:, :, :], ce[:, :, :], xs[:, 9:10, :].broadcast_to([P, HG, T]), ALU.mult
                        ).then_inc(S("cem"), 1)
        v.wait_ge(k, 7)
        v.wait_ge(S("cout_s"), NXC)
        v.wait_ge(S("xd"), ND)
        for c in range(NC + 1):
            n = P if c < NC else 32
            sl = slice(c * P, c * P + n)
            v.wait_ge(S("cb"), c + 1)
            v.tensor_copy(CB[0:n, :, 0:n], PS[0:n, 4, 0:NG * P].rearrange("p (g l) -> p g l", g=NG)[:, :, 0:n]
                          ).then_inc(S("cbc"), 1)
            if c >= 1:
                v.wait_ge(S("stm"), c)
            v.tensor_tensor(Bw[0:n, :, :].rearrange("p (g j) s -> p g j s", g=NG),
                            xtm[0:n, c, 1024:1152].rearrange("p (g s) -> p g s", g=NG).unsqueeze(2)
                            .broadcast_to([n, NG, HG, NS]),
                            wtm[0:n, c, :].rearrange("p (g j) -> p g j", g=NG).unsqueeze(3)
                            .broadcast_to([n, NG, HG, NS]), ALU.mult).then_inc(S("bwd"), 1)
            v.wait_ge(S("cbc"), c + 1)
            if c >= 1:
                v.wait_ge(S("ymm"), 2 * c)
            for hd in range(NH):
                v.wait_ge(S("lexp"), NH * c + hd + 1)
                v.scalar_tensor_tensor(out=SC[0:n, hd, 0:n], in0=L[0:n, hd, 0:n], scalar=dtm[0:n, c, hd:hd + 1],
                                       in1=CB[0:n, hd // HG, 0:n], op0=ALU.mult, op1=ALU.mult
                                       ).then_inc(S("scs"), 1)
            for b in range(2):
                v.wait_ge(S("ymm"), 2 * c + b + 1)
                v.tensor_tensor(ys[:, 4 * b:4 * b + 4, sl], xs[:, 4 * b:4 * b + 4, sl],
                                PS[:, 5 + b, :].rearrange("p (t l) -> p t l", t=4)[:, :, 0:n], ALU.add
                                ).then_inc(S("yad"), 1)
            if c < NC:
                v.wait_ge(S("stm"), c + 1)
                new = PS[:, 7, :].rearrange("p (j d) -> p j d", j=HG)
                st3 = ST[:, :].rearrange("p (j d) -> p j d", j=HG)
                if c == 0:
                    v.tensor_copy(st3, new).then_inc(S("stu"), 2)
                else:
                    v.wait_ge(S("stu"), 2 * c)
                    v.tensor_tensor(st3, st3, dec[:, :, c:c + 1].broadcast_to([P, HG, HD]), ALU.mult
                                    ).then_inc(S("stu"), 1)
                    v.wait_ge(S("stu"), 2 * c + 1)
                    v.tensor_tensor(st3, st3, new, ALU.add).then_inc(S("stu"), 1)
        for j in range(HG):
            for g in range(NG):
                hd = g * HG + j
                if j >= 1:
                    v.wait_ge(S("stm"), NC + 2 * (j - 1) + g + 1)
                v.tensor_tensor(XM[:, g, :, :],
                                xtm[0:32, NC, hd * HD:(hd + 1) * HD].unsqueeze(1).broadcast_to([32, NB, HD]),
                                seg[:, :].unsqueeze(2).broadcast_to([32, NB, HD]), ALU.mult
                                ).then_inc(S("xmd"), 1)
            if j == 0:
                v.wait_ge(S("s0_in"), 16)
            v.tensor_tensor(s0s[:, j, :, :], s0s[:, j, :, :],
                            dec[:, j, NC:].unsqueeze(2).broadcast_to([P, NB, HD]), ALU.mult
                            ).then_inc(S("st_s"), 1)
            v.wait_ge(S("stm"), NC + 2 * (j + 1))
            v.wait_ge(S("st_s"), 2 * j + 1)
            v.tensor_tensor(s0s[:, j, :, :], s0s[:, j, :, :],
                            PS[:, j % 2, :].rearrange("p (b d) -> p b d", b=NB), ALU.add
                            ).then_inc(S("st_s"), 1)
        v.wait_ge(S("yad"), 2 * (NC + 1))
        v.tensor_tensor(ys[:, :, :], ys[:, :, :], sz[:, :, :], ALU.mult).then_inc(S("ys_done"), 1)
        sh.norm_dve(v, 1, ys, ys, "norm_ssd", rstd)
        sh.norm_dve(v, 2, xl, xl, "norm_lru", rstd)
        with v.Fori(0, ND // 2) as i:
            for s in range(2):
                v.wait_ge(S("mm"), i * 2 + (O0 + s + 1))
                hs = h[:, ds(i * 2 + s, 1), :].rearrange("p a (h n) -> p (a h) n", h=2)
                v.tensor_tensor(hs, hs, pair(s), ALU.add).then_inc(S("pf0" if s == 0 else "pf1"), 1)

    return sync, pool, tensor, scalar, vector


def experts(nc, sh, w_q, keys, ut, vn, un):
    S, PS, pair, h, ident = sh.sem, sh.PS, sh.pair, sh.h, sh.ident

    def after_mixer(e):
        for name, n in (("pf0", MIX_TILES // 2 + 1), ("pf1", MIX_TILES // 2 + 1), ("out_s", 16 * 4)):
            e.wait_ge(S(name), n)

    (gd, idx8, dots, coef, xtok, yacc), KEEP = plan(
        nc, sh.free, ("gd", [P, IDS], F32), ("idx8", [P, 8], U32), ("dots", [P, IDS], F32), ("coef", [P, IDS], F32),
        ("xtok", [P, D], F32), ("yacc", [P, D], F32))
    (idxU,), KEEP = plan(nc, KEEP, ("idxU", [P, IDS], U32))
    (Xh, Xl), KEEP2 = plan(nc, KEEP, ("Xh", [P, ND, DT], F32R), ("Xl", [P, ND, DT], F32R))
    (xf, sq, rstd, W, qT, kT, tk, tr, cand, crep, m16, i16, b16, p16, pos, best, itop), e1 = plan(
        nc, KEEP2, ("xf", [P, ND, T], F32), ("sq_f", [P, 2, T], F32), ("rstd_f", [P, T], F32),
        ("wq_ring", [P, 2, ND, P], F32), ("qT", [P, 2, T], F32),
        ("kT", [P, 2 * PH, PK], F32), ("tk", [P, 2, NBK, 2, PK], F32), ("tr", [P, NBK, 2, PK], F32),
        ("cand", [P, NBK, TK * TK], F32), ("crep", [P, NBK, TK * TK], F32), ("m16", [P, NBK, 2, TK], F32),
        ("i16", [P, NBK, 2, TK], U32), ("b16", [P, NBK, TK], F32), ("p16", [P, NBK, TK], U32),
        ("pos", [P, NBK, PH, TK], U32), ("best", [P, NBK, PH, TK], F32), ("itop", [P, NBK, PH, 2, TK], BF16))
    (it16, E, ab_u, ab_f, gs, gm), e2 = plan(
        nc, e1, ("it16", [P, TK], BF16), ("E", [P, IDS, TK], BF16), ("ab_u", [P, 2, 2, IDS], U32),
        ("ab_f", [P, 2, 2, IDS], BF16), ("gs", [P, 2, 3, IDS], F32), ("gm", [P, 2, NBK * PH], F32))
    (stg,), e3 = plan(nc, KEEP2, ("stg", [P, 2, PK, GT_], F32))
    (ijg, iota, Aoh, oh), e3 = plan(nc, max(e3, e2), ("ijg", [P, 3, T], F32), ("iota", [P, PK], F32),
                                         ("Aoh", [P, 4, 4, PK], F32),
                                         ("oh", [P, 4, 2, 4, PK], F32))
    (Ur, Uh, Ul, Vr, Vh, Vl, Hh, Hl, hf, ge, G, ug, ix, d8), e4 = plan(
        nc, KEEP2, ("Ur", [P, 2, ND, P], F32), ("Uh", [P, GR, ND, P], F32R), ("Ul", [P, GR, ND, P], F32R),
        ("Vr", [P, 2, D], F32), ("Vh", [P, GR, D], F32R), ("Vl", [P, GR, D], F32R),
        ("Hh", [P, 2, GR, DT], F32R), ("Hl", [P, 2, GR, DT], F32R), ("hf", [P, 2, DT], F32),
        ("ge", [P, 2, DT], F32), ("G", [P, 2, GB, GR * GT_], F32), ("ug", [P, 4, D], F32),
        ("ix", [P, 2, 8], U32), ("d8", [P, 2, 8], F32))
    gates = nc.dram_tensor("gates", [GB, P, PK, GT_], F32, kind="Internal").ap()
    def need(e, name, v):
        if not isinstance(v, int) or v > 0:
            e.wait_ge(S(name), v)

    def num(i, s, per, k):
        return per * s + k if i is None else i * (2 * per) + (per * s + k)

    def blk_tok(b):
        return (b * P, P if b < NBK - 1 else T - (NBK - 1) * P)
    NTK = 79

    def sync(sp):
        after_mixer(sp)
        for s in range(2):
            sp.sem_inc(S("gw%d" % s), 16)
        sp.dma_start(kT[:, :, :], keys).then_inc(S("keys_in"), 16)
        for s in range(2):
            sp.dma_start(W[:, s, :, :], w_q[s, :, :, :]).then_inc(S("wq%d" % s), 16)
        with sp.Fori(0, PH - 1) as i:
            for s in range(2):
                sp.wait_ge(S("qmm"), i * 2 + (s + 1))
                sp.dma_start(W[:, s, :, :], w_q[ds(i * 2 + (s + 2), 1), :, :, :].rearrange("a p k m -> p (a k) m")
                             ).then_inc(S("wq%d" % s), 16)
        def load_u(i, g, c):
            q = c % 2
            need(sp, "uhi", num(i, g, GR, c - 1))
            need(sp, "ulo", num(i, g, GR, c - 1))
            sp.dma_start(Ur[:, q, :, :], ut[ds(num(i, g, GR, c), 1), :, :, :].rearrange("a p k j -> p (a k) j")
                         ).then_inc(S("ur%d" % q), 16)

        def load_v(i, g, c):
            q = c % 2
            need(sp, "vhi", num(i, g, GR, c - 1))
            need(sp, "vlo", num(i, g, GR, c - 1))
            sp.dma_start(Vr[:, q, :], vn[ds(num(i, g, GR * P, c * P), P), :]).then_inc(S("vr%d" % q), 16)

        def load_g(i, g):
            need(sp, "hfd", num(i, g, GR, -GR))
            sp.dma_start(G[:, g % 2, :, :], gates[:, :, ds(num(i, g, GR, 0), GR), :]
                         .rearrange("b p i t -> p b (i t)")).then_inc(S("gi%d" % (g % 2)), 16)

        for b in range(GB):
            if b == GB - 1:
                sp.wait_ge(S("gw0"), 16 * (GB // 2 + 1))
                for c in range(2):
                    load_u(None, 0, c)
            sp.wait_ge(S("gev"), 2 + (GT_ // 4) * (b + 1))
            sp.dma_start(gates[b, :, :, :], stg[:, b % 2, :, :]).then_inc(S("gw%d" % (b % 2)), 16)
        for c in range(2, GR):
            load_u(None, 0, c)
        sp.wait_ge(S("gw1"), 16 * (GB // 2 + 1))
        load_g(None, 0)
        for c in range(GR):
            load_u(None, 1, c)

        def step(i, g, last=False):
            if not last:
                load_g(i, g + 1)
            for c in range(GR):
                load_v(i, g, c)
            if not last and last is not None:
                for c in range(GR):
                    load_u(i, g + 2, c)
        for g in range(2):
            step(None, g)
        with sp.Fori(1, NGR // 2 - 1) as i:
            for s in range(2):
                step(i, s)
        step(None, NGR - 2, None)
        step(None, NGR - 1, True)

    def pool(p):
        after_mixer(p)
        p.memset(tk[:, :, NBK - 1, :, :], 0.0).then_inc(S("cst"), 1)
        p.iota(it16[:, :], [[1, TK]], base=0, channel_multiplier=0, allow_small_or_imprecise_dtypes=True
               ).then_inc(S("cst"), 1)
        p.iota(iota[:, :], [[1, PK]], base=0, channel_multiplier=0, allow_small_or_imprecise_dtypes=True
               ).then_inc(S("cst"), 1)
        p.memset(yacc[:, :], 0.0).then_inc(S("cst"), 1)
        p.wait_ge(S("gtc"), NBK)
        with p.Fori(0, DT // 16) as i:
            for q in range(4):
                p.wait_ge(S("dvo"), i * 4 + (q + 1))
                p.sem_inc(S("p_past"), 1)
                p.tensor_tensor(Aoh[:, q, :, :], oh[:, q, 0, :, :],
                                ijg[:, 2, ds(i * 16 + (SP_T + 4 * q), 4)].unsqueeze(2).broadcast_to([P, 4, PK]),
                                ALU.mult).then_inc(S("gated"), 1)
        p.wait_ge(S("gmm"), 4 + DT // 4)
        p.wait_ge(S("gev"), 2 + DT // 4)
        for s in range(2):
            p.wait_ge(S("gw%d" % s), 16 * (GB // 2 + 1))

        def fetch(i, g, src, g0):
            p.wait_ge(S("sdt"), num(i, g, 8, 0))
            p.tensor_copy(ix[:, g % 2, :], idxU[:, ds(num(i, g, 8, -8 * g0), 8)]).then_inc(S("ixc"), 1)
            p.wait_ge(S("ixc"), num(i, g, 1, 1))
            p.sem_inc(S("p_past"), 1)
            for u in range(8):
                p.wait_ge(S("sdt"), num(i, g, 8, u + 5))
                p.sem_inc(S("p_past"), 1)
                p.indirect_dma_start(out=ug[:, u % 4, :], out_offset=None, in_=src,
                                     in_offset=bass.IndirectOffsetOnAxis(ap=ix[:, g % 2, u:u + 1], axis=0)
                                     ).then_inc(S("gt%d" % (u % 4)), 16)
        with p.Fori(0, NGR // 4) as i:
            for s in range(2):
                fetch(i, s, un, 0)
        with p.Fori(0, NGR // 4) as i:
            for s in range(2):
                fetch(i, NGR // 2 + s, vn, NGR // 2)

    def tensor(pe):
        pe.sem_inc(S("scm"), 2)
        pe.sem_inc(S("vmm"), ND)
        sh.norm_pe(pe, 3, sq)
        pe.wait_ge(S("normed"), 4 * ND)
        pe.wait_ge(S("keys_in"), 16)
        for k in range(ND):
            m = pe.transpose(PS[:, 4 + k // 4, (k % 4) * P:(k % 4 + 1) * P], xf[:, k, 0:P], ident[:, :])
        m.then_inc(S("xt"), 1)
        pe.wait_ge(S("xtc"), 2)
        with pe.Fori(0, PH) as i:
            for s in range(2):
                pe.wait_ge(S("wq%d" % s), i * 16 + 16)
                pe.wait_ge(S("qev"), i * 2 + (s + 1))
                for k in range(ND):
                    for q in range(2):
                        m = pe.matmul(pair(s)[:, q, :], W[:, s, k, :], xf[:, k, q * HT:(q + 1) * HT],
                                      start=(k == 0), stop=(k == ND - 1))
                m.then_inc(S("qmm"), 1)
            for s in range(2):
                pe.wait_ge(S("qev"), i * 2 + (s + 3))
                pe.wait_ge(S("tkc"), i * 4 + (2 * s + 2))
                for b in range(NBK):
                    t0, w = blk_tok(b)
                    m = pe.matmul(PS[0:w, 4 + 2 * s + b // 4, (b % 4) * PK:(b % 4 + 1) * PK],
                                  qT[:, s, t0:t0 + w], kT[:, ds(i * 2 + s, 1), :].rearrange("p a k -> p (a k)"), start=True, stop=True)
                m.then_inc(S("scm"), 1)
        for b in range(NBK):
            t0, w = blk_tok(b)
            pe.wait_ge(S("sx"), b + 1)
            if b >= 2:
                pe.wait_ge(S("gtc"), b - 1)
            for q in range(3):
                m = pe.transpose(PS[:, b % 2, q * P:q * P + w], gs[0:w, b % 2, q, :], ident[0:w, 0:w])
            m.then_inc(S("gtp"), 1)
        pe.wait_ge(S("gtc"), NBK)
        pe.sem_inc(S("gmm"), 4)
        with pe.Fori(0, DT // 16) as i:
            for q in range(4):
                pe.wait_ge(S("gated"), i * 4 + (q + 1))
                pe.wait_ge(S("gev"), i * 4 + (q + 1))
                for u in range(4):
                    m = pe.matmul(PS[:, q % 2, u * PK:(u + 1) * PK], oh[:, q, 1, u, :], Aoh[:, q, u, :],
                                  start=True, stop=True)
                m.then_inc(S("gmm"), 1)
        pe.wait_ge(S("gev"), 2 + DT // 4)

        def phase_u(i, g):
            for c in range(GR):
                need(pe, "ulo", num(i, g, GR, c + 1))
                need(pe, "glu", num(i, g, GR, c - 3))
                out = PS[:, c, 0:DT]
                for k in range(ND):
                    pe.matmul(out, Uh[:, c, k, :], Xh[:, k, :], start=(k == 0), stop=False)
                    pe.matmul(out, Uh[:, c, k, :], Xl[:, k, :], start=False, stop=False)
                    m = pe.matmul(out, Ul[:, c, k, :], Xh[:, k, :], start=False, stop=(k == ND - 1))
                m.then_inc(S("umm"), 1)

        def phase_v(i, g):
            need(pe, "hlo", num(i, g, GR, GR))
            need(pe, "vlo", num(i, g, GR, GR))
            q = g % 2
            for d in range(ND):
                need(pe, "add", num(i, g, ND, d + 1))
                out = PS[:, 4 + d % 4, 0:DT]
                for c in range(GR):
                    w = slice(d * P, (d + 1) * P)
                    pe.matmul(out, Vh[:, c, w], Hh[:, q, c, :], start=(c == 0), stop=False)
                    pe.matmul(out, Vh[:, c, w], Hl[:, q, c, :], start=False, stop=False)
                    m = pe.matmul(out, Vl[:, c, w], Hh[:, q, c, :], start=False, stop=(c == GR - 1))
                m.then_inc(S("vmm"), 1)
        pe.wait_ge(S("xs"), 2 * ND)
        phase_u(None, 0)
        with pe.Fori(0, NGR // 2 - 1) as i:
            for s in range(2):
                phase_u(i, s + 1)
                phase_v(i, s)
        phase_u(None, NGR - 1)
        phase_v(None, NGR - 2)
        phase_v(None, NGR - 1)
        pe.wait_ge(S("sdt"), 2 * IDS + 8)
        for k in range(ND):
            m = pe.transpose(PS[:, k // 4, (k % 4) * P:(k % 4 + 1) * P], yacc[:, k * P:(k + 1) * P], ident[:, :])
        m.then_inc(S("fin"), 1)

    def scalar(a):
        a.sem_inc(S("tkc"), 4)
        a.sem_inc(S("qev"), 2)
        after_mixer(a)
        sh.norm_act(a, 3, h, sq, rstd)
        a.wait_ge(S("normed"), 4 * ND)
        a.wait_ge(S("cst"), 4)
        for k in range(ND):
            a.copy(Xh[:, k, :], xf[:, k, SP_T:T]).then_inc(S("xs"), 1)
        a.wait_ge(S("xt"), 1)
        for q in range(2):
            a.copy(xtok[:, q * 512:(q + 1) * 512], PS[:, 4 + q, :]).then_inc(S("xtc"), 1)
        with a.Fori(0, PH // 2) as i:
            for hp in range(2):
                for s in range(2):
                    n = 2 * hp + s
                    a.wait_ge(S("qmm"), i * 4 + (n + 1))
                    a.wait_ge(S("scm"), i * 4 + (n + 1))
                    a.copy(halves(qT[:, s, :]), pair(s)).then_inc(S("qev"), 1)
                for s in range(2):
                    n = 2 * hp + s
                    a.wait_ge(S("scm"), i * 4 + (n + 3))
                    a.wait_ge(S("tkd"), i * 2 + (hp + 1))
                    a.copy(tk[:, hp, 0:4, s, :], PS[:, 4 + 2 * s, :].rearrange("p (b k) -> p b k", b=4)
                           ).then_inc(S("tkc"), 1)
                    a.copy(tk[0:32, hp, 4, s, :], PS[0:32, 5 + 2 * s, 0:PK]).then_inc(S("tkc"), 1)
        a.preload_act_table(ACT.Exp)
        a.wait_ge(S("dc"), 1)
        a.activation(best[:, :, :, :].rearrange("p b h k -> p b (h k)"), crep[:, :, 0:IDS], ACT.Exp).then_inc(S("cf"), 1)
        for b in range(NBK):
            t0, w = blk_tok(b)
            a.wait_ge(S("gtp"), b + 1)
            a.copy(ijg[:, :, t0:t0 + w], PS[:, b % 2, 0:3 * P].rearrange("p (q t) -> p q t", q=3)[:, :, 0:w]
                   ).then_inc(S("gtc"), 1)
        a.sem_inc(S("gev"), 2)
        with a.Fori(0, GB // 2) as bb:
            for s in range(2):
                if s == 0:
                    a.wait_ge(S("gw0"), bb * 16 + 16)
                else:
                    a.wait_ge(S("gw1"), bb * 16 + 16)
                with a.Fori(0, GT_ // 8) as i:
                    for q in range(2):
                        a.wait_ge(S("gmm"), bb * 52 + i * 2 + (26 * s + q + 5))
                        a.copy(stg[:, s, :, ds(i * 8 + 4 * q, 4)].rearrange("p i t -> p t i"),
                               PS[:, q, :].rearrange("p (t i) -> p t i", t=4)).then_inc(S("gev"), 1)
        a.preload_act_table(ACT.Gelu_apprx_tanh)

        def split_u(i, g, c):
            need(a, "ur%d" % (c % 2), num(i, g, 32, 16 * (c // 2 + 1)))
            need(a, "umm", num(i, g, GR, c - 3))
            a.copy(Uh[:, c, :, :], Ur[:, c % 2, :, :]).then_inc(S("uhi"), 1)

        def split_v(i, g, c):
            need(a, "vr%d" % (c % 2), num(i, g, 32, 16 * (c // 2 + 1)))
            need(a, "vmm", num(i, g, ND, ND))
            a.copy(Vh[:, c, :], Vr[:, c % 2, :]).then_inc(S("vhi"), 1)

        def act_u(i, g, c):
            need(a, "umm", num(i, g, GR, c + 1))
            need(a, "hfd", num(i, g, GR, c - 1))
            a.activation(ge[:, c % 2, :], PS[:, c, 0:DT], ACT.Gelu_apprx_tanh).then_inc(S("glu"), 1)
            need(a, "hfd", num(i, g, GR, c + 1))
            need(a, "vmm", num(i, g, ND, 0))
            a.copy(Hh[:, g % 2, c, :], hf[:, c % 2, :]).then_inc(S("hhi"), 1)

        def step(i, g, u=True, nxt=True):
            for c in range(GR):
                split_v(i, g, c)
                if u:
                    act_u(i, g + 1, c)
            if nxt:
                for c in range(GR):
                    split_u(i, g + 2, c)
        a.wait_ge(S("gw0"), 16 * (GB // 2 + 1))
        for c in range(GR):
            split_u(None, 0, c)
        a.wait_ge(S("gw1"), 16 * (GB // 2 + 1))
        for c in range(GR):
            act_u(None, 0, c)
        for c in range(GR):
            split_u(None, 1, c)
        with a.Fori(0, NGR // 4) as i:
            for s in range(2):
                step(i, s)
        a.wait_ge(S("cf"), 2)
        a.activation(coef[:, :], dots[:, :], ACT.Gelu_apprx_tanh).then_inc(S("cf"), 1)
        with a.Fori(0, NGR // 4 - 1) as i:
            for s in range(2):
                step(i, s + NGR // 2)
        step(None, NGR - 2, True, False)
        step(None, NGR - 1, False, False)

    def vector(v):
        v.sem_inc(S("tkd"), 2)
        sh.norm_dve(v, 3, h, xf, "norm_ffn", rstd)
        v.wait_ge(S("xs"), ND)
        for k in range(ND):
            v.tensor_tensor(Xl[:, k, :], xf[:, k, SP_T:T], Xh[:, k, :].bitcast(F32), ALU.subtract
                            ).then_inc(S("xs"), 1)
        v.wait_ge(S("cst"), 4)
        tc = S("tc")
        LOW = -3.0e38
        NS_ = 2 * NBK
        sets = [(b, c) for b in range(NBK) for c in range(2)]
        with v.Fori(0, PH // 2) as i:
            for hp in range(2):
                def done(n):
                    v.wait_ge(tc, i * (2 * NTK) + (hp * NTK + n))
                    v.sem_inc(S("v_past"), 1)
                v.wait_ge(S("tkc"), i * 8 + (4 * hp + 8))
                v.sem_inc(S("v_past"), 1)
                for b, c in sets:
                    v.max(m16[:, b, c, 0:8], tk[:, hp, b, c, :]).then_inc(tc, 1)
                done(NS_)
                for b, c in sets:
                    v.max_index(i16[:, b, c, 0:8], m16[:, b, c, 0:8], tk[:, hp, b, c, :]).then_inc(tc, 1)
                for b, c in sets:
                    v.match_replace(tr[:, b, c, :], m16[:, b, c, 0:8], tk[:, hp, b, c, :], LOW).then_inc(tc, 1)
                done(3 * NS_)
                for b, c in sets:
                    v.max(m16[:, b, c, 8:16], tr[:, b, c, :]).then_inc(tc, 1)
                done(4 * NS_)
                for b, c in sets:
                    v.max_index(i16[:, b, c, 8:16], m16[:, b, c, 8:16], tr[:, b, c, :]).then_inc(tc, 1)
                v.tensor_tensor(cand[:, :, :].rearrange("p b (x y) -> p b x y", x=TK),
                                m16[:, :, 0, :].unsqueeze(3).broadcast_to([P, NBK, TK, TK]),
                                m16[:, :, 1, :].unsqueeze(2).broadcast_to([P, NBK, TK, TK]), ALU.add
                                ).then_inc(tc, 1)
                o_ = 5 * NS_ + 1
                done(o_)
                for b in range(NBK):
                    v.max(b16[:, b, 0:8], cand[:, b, :]).then_inc(tc, 1)
                done(o_ + NBK)
                for b in range(NBK):
                    v.max_index(p16[:, b, 0:8], b16[:, b, 0:8], cand[:, b, :]).then_inc(tc, 1)
                for b in range(NBK):
                    v.match_replace(crep[:, b, :], b16[:, b, 0:8], cand[:, b, :], LOW).then_inc(tc, 1)
                done(o_ + 3 * NBK)
                for b in range(NBK):
                    v.max(b16[:, b, 8:16], crep[:, b, :]).then_inc(tc, 1)
                done(o_ + 4 * NBK)
                for b in range(NBK):
                    v.max_index(p16[:, b, 8:16], b16[:, b, 8:16], crep[:, b, :]).then_inc(tc, 1)
                done(o_ + 5 * NBK)
                hs = ds(i * 2 + hp, 1)
                v.tensor_copy(pos[:, :, hs, :].rearrange("p b a k -> p b (a k)"), p16[:, :, :]).then_inc(tc, 1)
                v.tensor_copy(best[:, :, hs, :].rearrange("p b a k -> p b (a k)"), b16[:, :, :]).then_inc(tc, 1)
                v.tensor_copy(itop[:, :, hs, :, :].rearrange("p b a c k -> p b (a c) k"), i16[:, :, :, :]
                              ).then_inc(tc, 1)
                done(NTK)
                v.sem_inc(S("tkd"), 1)
        dc = S("dc")
        bf = best[:, :, :, :].rearrange("p b h k -> p (b h) k")
        v.tensor_tensor(crep[:, :, 0:IDS].rearrange("p b (h k) -> p b h k", h=PH), best[:, :, :, :],
                        best[:, :, :, 0:1].broadcast_to([P, NBK, PH, TK]), ALU.subtract).then_inc(dc, 1)
        v.wait_ge(S("cf"), 1)
        v.tensor_reduce(gm[:, 0, :], bf, AX.X, ALU.add).then_inc(dc, 1)
        v.wait_ge(dc, 2)
        v.reciprocal(gm[:, 1, :], gm[:, 0, :]).then_inc(dc, 1)
        v.wait_ge(dc, 3)
        v.tensor_tensor(bf, bf, gm[:, 1, :].unsqueeze(2).broadcast_to([P, NBK * PH, TK]), ALU.mult
                        ).then_inc(dc, 1)
        v.wait_ge(dc, 4)
        n = 4
        for b in range(NBK):
            r = b % 2
            if b >= 2:
                v.wait_ge(S("gtp"), b - 1)
            pf = pos[:, b, :, :].rearrange("p h k -> p (h k)")
            v.tensor_scalar(ab_u[:, r, 0, :], pf, 4, None, ALU.logical_shift_right).then_inc(dc, 1)
            v.tensor_scalar(ab_u[:, r, 1, :], pf, TK - 1, None, ALU.bitwise_and).then_inc(dc, 1)
            v.wait_ge(dc, n + 2)
            v.tensor_copy(ab_f[:, r, :, :], ab_u[:, r, :, :]).then_inc(dc, 1)
            v.tensor_copy(gs[:, r, 2, :], best[:, b, :, :].rearrange("p h k -> p (h k)")).then_inc(dc, 1)
            v.wait_ge(dc, n + 4)
            n += 4
            for q in range(2):
                v.tensor_tensor(E[:, :, :], ab_f[:, r, q, :].unsqueeze(2).broadcast_to([P, IDS, TK]),
                                it16[:, :].unsqueeze(1).broadcast_to([P, IDS, TK]), ALU.is_equal
                                ).then_inc(dc, 1)
                v.wait_ge(dc, n + 1)
                e4_ = E[:, :, :].rearrange("p (h k) x -> p h k x", h=PH)
                v.tensor_tensor(e4_, e4_, itop[:, b, :, q, :].unsqueeze(2).broadcast_to([P, PH, TK, TK]),
                                ALU.mult).then_inc(dc, 1)
                v.wait_ge(dc, n + 2)
                v.tensor_reduce(gs[:, r, q, :], E[:, :, :], AX.X, ALU.add).then_inc(dc, 1)
                v.wait_ge(dc, n + 3)
                n += 3
            if b == 0:
                v.scalar_tensor_tensor(out=idxU[:, :], in0=gs[:, 0, 0, :], scalar=float(PK), in1=gs[:, 0, 1, :],
                                       op0=ALU.mult, op1=ALU.add).then_inc(dc, 1)
                v.tensor_copy(gd[:, :], gs[:, 0, 2, :]).then_inc(dc, 1)
                n += 2
            v.wait_ge(dc, n)
            v.sem_inc(S("sx"), 1)
        v.wait_ge(S("gtc"), NBK)
        with v.Fori(0, DT // 16) as i:
            for q in range(4):
                v.wait_ge(S("gmm"), i * 4 + (q + 1))
                v.tensor_tensor(oh[:, q, :, :, :], iota[:, :].unsqueeze(1).unsqueeze(1).broadcast_to([P, 2, 4, PK]),
                                ijg[:, 0:2, ds(i * 16 + (SP_T + 4 * q), 4)].unsqueeze(3)
                                .broadcast_to([P, 2, 4, PK]), ALU.is_equal).then_inc(S("dvo"), 1)

        def split_u(i, g, c):
            need(v, "uhi", num(i, g, GR, c + 1))
            v.tensor_tensor(Ul[:, c, :, :], Ur[:, c % 2, :, :], Uh[:, c, :, :].bitcast(F32), ALU.subtract
                            ).then_inc(S("ulo"), 1)

        def split_v(i, g, c):
            need(v, "vhi", num(i, g, GR, c + 1))
            v.tensor_tensor(Vl[:, c, :], Vr[:, c % 2, :], Vh[:, c, :].bitcast(F32), ALU.subtract
                            ).then_inc(S("vlo"), 1)

        def gate_u(i, g, c):
            q = g % 2
            if c == 0:
                need(v, "gi%d" % q, num(i, g, 8, 16 - 8 * q))
            need(v, "glu", num(i, g, GR, c + 1))
            need(v, "hhi", num(i, g, GR, c - 1))
            need(v, "hlo", num(i, g, GR, c - 1))
            v.tensor_tensor(hf[:, c % 2, :].rearrange("p (b t) -> p b t", b=GB),
                            ge[:, c % 2, :].rearrange("p (b t) -> p b t", b=GB),
                            G[:, q, :, c * GT_:(c + 1) * GT_], ALU.mult).then_inc(S("hfd"), 1)
            need(v, "hhi", num(i, g, GR, c + 1))
            v.tensor_tensor(Hl[:, q, c, :], hf[:, c % 2, :], Hh[:, q, c, :].bitcast(F32), ALU.subtract
                            ).then_inc(S("hlo"), 1)

        def add_v(i, g, d):
            need(v, "vmm", num(i, g, ND, ND + d + 1))
            v.tensor_tensor(h[:, d, SP_T:T], h[:, d, SP_T:T], PS[:, 4 + d % 4, 0:DT], ALU.add
                            ).then_inc(S("add"), 1)

        def row(i, g, u, part):
            q = u % 4
            need(v, "gt%d" % q, num(i, g, 32, 16 * (u // 4 + 1)))
            if part == 0:
                v.tensor_tensor_reduce(ug[:, q, :], ug[:, q, :], xtok[:, :], 1.0, 0.0, ALU.mult, ALU.add,
                                       d8[:, g % 2, u:u + 1]).then_inc(S("sdt"), 1)
            else:
                need(v, "sdt", num(i, g, 8, u + 8))
                v.scalar_tensor_tensor(out=yacc[:, :], in0=ug[:, q, :],
                                       scalar=coef[:, ds(num(i, g, 8, u - IDS), 1)], in1=yacc[:, :],
                                       op0=ALU.mult, op1=ALU.add).then_inc(S("sdt"), 1)

        def step(i, g, part, u=True, nxt=True):
            for c in range(GR):
                split_v(i, g, c)
                if u:
                    gate_u(i, g + 1, c)
                row(i, g, c, part)
            for d in range(ND):
                add_v(i, g, d)
                if d % 2 == 1:
                    if nxt:
                        split_u(i, g + 2, d // 2)
                    row(i, g, GR + d // 2, part)
            if part == 0:
                v.wait_ge(S("sdt"), num(i, g, 8, 16))
                v.tensor_copy(dots[:, ds(num(i, g, 8, 0), 8)], d8[:, g % 2, :]).then_inc(S("fin2"), 1)
        v.sem_inc(S("add"), 4)
        v.sem_inc(S("sdt"), 8)
        for c in range(GR):
            split_u(None, 0, c)
        for c in range(GR):
            gate_u(None, 0, c)
        for c in range(GR):
            split_u(None, 1, c)
        with v.Fori(0, NGR // 4) as i:
            for s in range(2):
                step(i, s, 0)
        v.wait_ge(S("fin2"), NGR // 2)
        v.sem_inc(S("cf"), 1)
        v.wait_ge(S("cf"), 3)
        v.tensor_tensor(coef[:, :], coef[:, :], gd[:, :], ALU.mult).then_inc(S("cf"), 1)
        v.wait_ge(S("cf"), 4)
        with v.Fori(0, NGR // 4 - 1) as i:
            for s in range(2):
                step(i, s + NGR // 2, 1)
        step(None, NGR - 2, 1, True, False)
        step(None, NGR - 1, 1, False, False)
        v.wait_ge(S("fin"), 1)
        for k in range(ND):
            v.tensor_tensor(h[:, k, 0:P], h[:, k, 0:P], PS[:, k // 4, (k % 4) * P:(k % 4 + 1) * P], ALU.add
                            ).then_inc(S("fo"), 1)

    return sync, pool, tensor, scalar, vector


def closing(nc, sh, pT, w_ple, y):
    S, pair, h = sh.sem, sh.pair, sh.h
    (hn, mv, pe_in, W, gbuf, sq, rstd), _ = plan(
        nc, sh.free, ("hn", [P, ND, T], F32), ("mv", [P, ND, T], F32), ("pe_in", [P, KP, T], F32),
        ("w_ple_ring", [P, 2, ND + KP, P], F32), ("gbuf", [P, 2, T], F32), ("sq_c", [P, 2, T], F32),
        ("rstd_c", [P, T], F32))

    def sync(sp):
        sp.wait_ge(S("fo"), ND)
        sp.dma_start(pe_in[:, :, :], pT).then_inc(S("ple_in"), 16)
        for s in range(2):
            sp.dma_start(W[:, s, :, :], w_ple[s, :, :, :]).then_inc(S("wp%d" % s), 16)
        with sp.Fori(0, ND // 2 - 1) as i:
            for s in range(2):
                sp.wait_ge(S("plm"), i * 2 + (s + 1))
                sp.dma_start(W[:, s, :, :], w_ple[ds(i * 2 + (s + 2), 1), :, :, :].rearrange("a p k m -> p (a k) m")
                             ).then_inc(S("wp%d" % s), 16)
        for k in range(ND):
            sp.wait_ge(S("normed"), 6 * ND + k + 1)
            sp.dma_start(y[:, k, :], hn[:, k, :]).then_inc(S("y_out"), 16)
        sp.wait_ge(S("y_out"), 16 * ND)
        sp.wait_ge(S("out_s"), 16 * 4)

    def pool(p):
        pass

    def tensor(pe):
        sh.norm_pe(pe, 4, sq)
        pe.wait_ge(S("normed"), 5 * ND)
        pe.wait_ge(S("ple_in"), 16)
        with pe.Fori(0, ND // 2) as i:
            for s in range(2):
                pe.wait_ge(S("wp%d" % s), i * 16 + 16)
                pe.wait_ge(S("plg"), i * 2 + (s + 1))
                for k in range(ND):
                    for q in range(2):
                        pe.matmul(pair(s)[:, q, :], W[:, s, k, :], hn[:, k, q * HT:(q + 1) * HT],
                                  start=(k == 0), stop=(k == ND - 1))
                pe.wait_ge(S("plp"), i * 2 + (s + 1))
                for k in range(KP):
                    for q in range(2):
                        m = pe.matmul(pair(2 + s)[:, q, :], W[:, s, ND + k, :], pe_in[:, k, q * HT:(q + 1) * HT],
                                      start=(k == 0), stop=(k == KP - 1))
                m.then_inc(S("plm"), 1)
        pe.wait_ge(S("plp"), ND + 2)
        sh.norm_pe(pe, 5, sq)
        sh.norm_pe(pe, 6, sq)

    def scalar(a):
        a.wait_ge(S("fo"), ND)
        sh.norm_act(a, 4, h, sq, rstd)
        a.sem_inc(S("plg"), 2)
        a.preload_act_table(ACT.Sigmoid)
        with a.Fori(0, ND // 2) as i:
            for s in range(2):
                a.wait_ge(S("plm"), i * 2 + (s + 1))
                a.wait_ge(S("plp"), i * 2 + (s + 1))
                a.activation(halves(gbuf[:, s, :]), pair(s), ACT.Sigmoid).then_inc(S("plg"), 1)
        sh.norm_act(a, 5, mv, sq, rstd, "plp", 2)
        sh.norm_act(a, 6, h, sq, rstd, "res")

    def vector(v):
        v.wait_ge(S("fo"), ND)
        sh.norm_dve(v, 4, h, hn, "norm_plg", rstd)
        v.sem_inc(S("plp"), 2)
        with v.Fori(0, ND // 2) as i:
            for s in range(2):
                v.wait_ge(S("plg"), i * 2 + (s + 3))
                v.tensor_tensor(mv[:, ds(i * 2 + s, 1), :].rearrange("p a (h n) -> p (a h) n", h=2),
                                halves(gbuf[:, s, :]), pair(2 + s), ALU.mult).then_inc(S("plp"), 1)
        sh.norm_dve(v, 5, mv, mv, "norm_plo", rstd)
        for k in range(ND):
            v.wait_ge(S("normed"), 5 * ND + k + 1)
            v.tensor_tensor(h[:, k, :], h[:, k, :], mv[:, k, :], ALU.add).then_inc(S("res"), 1)
        sh.norm_dve(v, 6, h, hn, "norm_fin", rstd)

    return sync, pool, tensor, scalar, vector


def build(nc, x, w_xc, w_z, w_gate, w_dt, par, head, w_rg, w_ig, conv_in, s0, lru0, w_out, w_q, keys, ut, vn, un,
          pT, w_ple, y, ssd_p, ssd_s, conv_o, lru_o):
    with ExitStack() as ctx:
        sh = Shared(nc, ctx)
        stages = (mixer(nc, sh, x, w_xc, w_z, w_gate, w_dt, par, head, w_rg, w_ig, conv_in, s0, lru0, w_out,
                        ssd_p, ssd_s, conv_o, lru_o),
                  experts(nc, sh, w_q, keys, ut, vn, un),
                  closing(nc, sh, pT, w_ple, y))
        block = ctx.enter_context(nc.Block())

        @block.sync
        def _(sp):
            for stage in stages:
                stage[0](sp)

        @block.gpsimd
        def _(g):
            for stage in stages:
                stage[1](g)

        @block.tensor
        def _(pe):
            for stage in stages:
                stage[2](pe)

        @block.scalar
        def _(a):
            for stage in stages:
                stage[3](a)

        @block.vector
        def _(v):
            for stage in stages:
                stage[4](v)


def layout(i):
    import numpy as np
    g = {k: np.asarray(v) for k, v in i.items()}
    fm = lambda a: np.ascontiguousarray(a.T.reshape(-1, P, a.shape[0]).transpose(1, 0, 2))
    tiles = lambda w: np.ascontiguousarray(
        w.reshape(w.shape[0] // P, P, w.shape[1] // P, P).transpose(2, 1, 0, 3))
    vec = lambda a: a.reshape(-1, P).T
    d = {}
    d["x"] = fm(np.concatenate([g["x_prompt"][0], g["x_sample"].reshape(-1, D)]))
    w = g["w_in"][0]
    s1, s2 = D, D + NXS * P
    s3, s4 = s2 + NH, s2 + NH + D
    d["w_xc"] = tiles(np.concatenate([w[:, s1:s2], w[:, s4:]], axis=1))
    d["w_z"] = tiles(w[:, :s1])
    d["w_gate"] = tiles(w[:, s3:s4])
    d["w_dt"] = np.ascontiguousarray(w[:, s2:s3].reshape(ND, P, NH).transpose(1, 0, 2))
    cw = np.concatenate([g["conv_ssd_w"][0], g["conv_lru_w"][0]], axis=1)
    cb = np.concatenate([g["conv_ssd_b"][0], g["conv_lru_b"][0]])
    d["par"] = np.ascontiguousarray(np.concatenate(
        [vec(g["norm_mix"][0])] + [vec(cw[k]) for k in range(CW)] + [vec(cb)]
        + [vec(g[n][0]) for n in ("norm_ssd", "b_rgate", "b_igate", "lru_lambda", "norm_lru", "norm_ffn",
                                  "norm_ple_gate", "norm_ple_out")]
        + [vec(g["norm_final"]), vec(np.repeat(g["d_skip"][0], HD))], axis=1))
    d["head"] = np.ascontiguousarray(np.stack([g["dt_bias"][0], g["a_log"][0]], axis=1))
    d["w_rg"] = g["w_rgate"][0].reshape(ND, 2, 64, 64)
    d["w_ig"] = g["w_igate"][0].reshape(ND, 2, 64, 64)
    ci = np.concatenate([g["state_ssd_conv"][0], g["state_lru_conv"][0]], axis=2)
    d["conv_in"] = np.ascontiguousarray(ci.reshape(NB, CW - 1, NXC, P).transpose(3, 2, 0, 1))
    s = g["state_ssd"][0].reshape(NB, NG, HG, HD, NS)
    d["s0"] = np.ascontiguousarray(s.transpose(1, 4, 2, 0, 3).reshape(P, HG, NB, HD))
    d["lru0"] = np.ascontiguousarray(g["state_lru"][0].reshape(NB, ND, P).transpose(2, 1, 0))
    d["w_out"] = tiles(g["w_out"][0])
    d["w_q"] = tiles(g["peer_wq"][0])
    d["keys"] = np.ascontiguousarray(g["peer_keys"][0].reshape(2 * PH, PK, P).transpose(2, 0, 1))
    u = g["peer_u"][0]
    d["ut"] = np.ascontiguousarray(u.reshape(PK, PK, ND, P).transpose(0, 3, 2, 1))
    d["un"], d["vn"] = u, g["peer_v"][0]
    d["pT"] = fm(np.concatenate([g["p_prompt"][0, 0], g["p_sample"][0].reshape(NB * LB, KP * P)]))
    d["w_ple"] = np.ascontiguousarray(np.concatenate(
        [tiles(g["w_ple_gate"][0]), tiles(g["w_ple_proj"][0])], axis=2))
    return d


OUTS = {"y": (P, ND, T), "ssd_p": (P, HG * HD), "ssd_s": (P, HG, NB, HD), "conv_o": (P, NXC, 27),
        "lru_o": (P, ND, 1 + NB)}


def kernel(**inputs):
    import numpy as np
    import concourse.bacc as bacc
    from concourse.bass_utils import run_bass_kernel_spmd as run
    d = layout(inputs)
    nc = bacc.Bacc("TRN2", target_bir_lowering=False, num_devices=1)
    args = {n: nc.dram_tensor(n, a.shape, mybir.dt.from_np(a.dtype), kind="ExternalInput").ap() for n, a in d.items()}
    args |= {n: nc.dram_tensor(n, s, F32, kind="ExternalOutput").ap() for n, s in OUTS.items()}
    build(nc, **args)
    r = run(nc, [d], core_ids=[0]).results[0]
    y = r["y"].transpose(2, 1, 0).reshape(T, D)
    ssd_state_p = r["ssd_p"].reshape(NG, NS, HG, HD).transpose(0, 2, 3, 1).reshape(1, 1, NH, HD, NS)
    ssd_state_s = r["ssd_s"].reshape(NG, NS, HG, NB, HD).transpose(3, 0, 2, 4, 1).reshape(1, NB, NH, HD, NS)
    co, lo = r["conv_o"], r["lru_o"]
    cp = co[:, :, 0:CW - 1].transpose(2, 1, 0).reshape(1, 1, CW - 1, NXC * P)
    cs = co[:, :, CW - 1:].reshape(P, NXC, NB, CW - 1).transpose(2, 3, 1, 0).reshape(1, NB, CW - 1, NXC * P)
    s = NXS * P
    return tuple(np.ascontiguousarray(a) for a in (
        y[:NP].reshape(1, NP, D), y[NP:].reshape(NB, LB, D),
        ssd_state_p, cp[..., :s], lo[:, :, 0].T.reshape(1, 1, D), cp[..., s:],
        ssd_state_s, cs[..., :s], lo[:, :, 1:].transpose(2, 1, 0).reshape(1, NB, D), cs[..., s:]))
```
